# Optimizing a Trainium2 kernel written in Bass

```python
import jax
import jax.numpy as jnp
from jax import lax
import numpy as np

D_MODEL = 1024
BATCH = 1
SEQ = 1024
DEPTH = 1

CHUNK = 64
HEAD_DIM = 64
A_HEADS = 8
A_KV_HEADS = 2
A_GROUP = A_HEADS // A_KV_HEADS
A_WINDOW = 128
A_WIN_CHUNKS = A_WINDOW // CHUNK
REL_BUCKETS = 32
REL_MAX_DIST = 128
B_HEADS = 4
B_KEY_DIM = 64
B_VAL_DIM = 64
C_HEADS = 4
C_HEAD_DIM = 64
C_GROUPS = 2
C_STATE = 64
C_CONV = 4
D_HEADS = 4
D_QBLOCK = 128
N_BRANCH = 4

A_Q_W = A_HEADS * HEAD_DIM
A_KV_W = A_KV_HEADS * HEAD_DIM
B_K_W = B_HEADS * B_KEY_DIM
B_V_W = B_HEADS * B_VAL_DIM
C_INNER = C_HEADS * C_HEAD_DIM
C_BC_W = C_GROUPS * C_STATE
C_CONV_DIM = C_INNER + 2 * C_BC_W
D_W = D_HEADS * HEAD_DIM
IN_SPLITS = (A_Q_W, A_KV_W, A_KV_W, B_K_W, B_K_W, B_V_W, B_V_W, C_INNER, C_CONV_DIM, C_HEADS, D_W, D_W, D_W, D_HEADS, N_BRANCH * D_MODEL)
D_IN = sum(IN_SPLITS)

N_EXPERTS = 64
N_EXPERT_GROUPS = 8
TOPK_GROUPS = 4
TOP_K = 6
EXPERT_FF = 256
SHARED_FF = 256
ROUTED_SCALE = 2.5
MOE_BLOCK = 128
MOE_BLOCKS_PER_STEP = 8

DEEPNORM_ALPHA = (2.0 * DEPTH) ** 0.25
DEEPNORM_BETA = (8.0 * DEPTH) ** -0.25
LN_EPS = 1e-5
RMS_EPS = 1e-6
F32 = jnp.float32

kernel_name = 'hybrid_gated_swa_hgrn2_ssd_fox_moe_deepnorm'

def layer_norm(x, g, b):
    xf = x.astype(F32)
    mu = jnp.mean(xf, axis=-1, keepdims=True)
    var = jnp.mean(jnp.square(xf - mu), axis=-1, keepdims=True)
    return ((xf - mu) * lax.rsqrt(var + LN_EPS) * g + b).astype(x.dtype)

def rms_norm(x, g):
    xf = x.astype(F32)
    return xf * lax.rsqrt(jnp.mean(jnp.square(xf), axis=-1, keepdims=True) + RMS_EPS) * g

def segsum(x):
    t = x.shape[-1]
    xr = jnp.broadcast_to(x[..., :, None], x.shape + (t,))
    strict = jnp.tril(jnp.ones((t, t), dtype=bool), -1)
    ss = jnp.cumsum(jnp.where(strict, xr, 0.0), axis=-2)
    return jnp.where(jnp.tril(jnp.ones((t, t), dtype=bool)), ss, -jnp.inf)

def t5_band_buckets():
    t = np.arange(CHUNK)[:, None]
    j = np.arange(A_WIN_CHUNKS * CHUNK)[None, :]
    rel = j - (A_WIN_CHUNKS - 1) * CHUNK - t
    nb = REL_BUCKETS // 2
    max_exact = nb // 2
    n = np.abs(rel)
    large = max_exact + (np.log(np.maximum(n, 1) / max_exact) / np.log(REL_MAX_DIST / max_exact) * (nb - max_exact)).astype(np.int32)
    large = np.minimum(large, nb - 1)
    bucket = (rel > 0).astype(np.int32) * nb + np.where(n < max_exact, n, large)
    return bucket.astype(np.int32)

def t5_band_bias(rel_bias):
    bias = rel_bias.astype(F32)[t5_band_buckets()]
    return bias.transpose(2, 0, 1).reshape(A_KV_HEADS, A_GROUP, CHUNK, A_WIN_CHUNKS * CHUNK)

def swa_sink_attention(q, k, v, sinks, bias):
    bsz, seq = q.shape[:2]
    nc = seq // CHUNK
    kw = A_WIN_CHUNKS * CHUNK
    qc = q.astype(F32).reshape(bsz, nc, CHUNK, A_KV_HEADS, A_GROUP, HEAD_DIM)
    kc = k.astype(F32).reshape(bsz, nc, CHUNK, A_KV_HEADS, HEAD_DIM)
    vc = v.astype(F32).reshape(bsz, nc, CHUNK, A_KV_HEADS, HEAD_DIM)
    pad = ((0, 0), (A_WIN_CHUNKS - 1, 0), (0, 0), (0, 0), (0, 0))
    kp = jnp.pad(kc, pad)
    vp = jnp.pad(vc, pad)
    kb = jnp.concatenate([kp[:, i:i + nc] for i in range(A_WIN_CHUNKS)], axis=2)
    vb = jnp.concatenate([vp[:, i:i + nc] for i in range(A_WIN_CHUNKS)], axis=2)
    s = jnp.einsum('bnqhgd,bnkhd->bnhgqk', qc, kb) * HEAD_DIM ** -0.5 + bias
    key_pos = jnp.arange(nc)[:, None] * CHUNK + jnp.arange(kw)[None, :] - (A_WIN_CHUNKS - 1) * CHUNK
    s = jnp.where((key_pos >= 0)[None, :, None, None, None, :], s, -jnp.inf)
    sink = sinks.astype(F32).reshape(1, 1, A_KV_HEADS, A_GROUP, 1, 1)
    m = jnp.maximum(jnp.max(s, axis=-1, keepdims=True), sink)
    p = jnp.exp(s - m)
    denom = jnp.sum(p, axis=-1, keepdims=True) + jnp.exp(sink - m)
    o = jnp.einsum('bnhgqk,bnkhd->bnqhgd', p / denom, vb)
    return o.reshape(bsz, seq, A_Q_W)

def hgrn2_mixer(q, f_raw, i_in, g, lb, norm_w):
    bsz, seq = q.shape[:2]
    nc = seq // CHUNK
    fgate = lb + (1.0 - lb) * jax.nn.sigmoid(f_raw.astype(F32))
    logf = jnp.log(fgate)
    key = 1.0 - fgate

    def chunks(t, d):
        return t.reshape(bsz, nc, CHUNK, B_HEADS, d).transpose(1, 0, 3, 2, 4)

    qs = chunks(q.astype(F32), B_KEY_DIM)
    ks = chunks(key, B_KEY_DIM)
    gs = chunks(logf, B_KEY_DIM)
    vs = chunks(i_in.astype(F32), B_VAL_DIM)
    causal = jnp.tril(jnp.ones((CHUNK, CHUNK), dtype=bool))

    def step(state, inp):
        qc, kc, vc, gc = inp
        b = jnp.cumsum(gc, axis=2)
        o_inter = jnp.einsum('bhtk,bhkv->bhtv', qc * jnp.exp(b), state)
        diff = b[:, :, :, None, :] - b[:, :, None, :, :]
        decay = jnp.exp(jnp.where(causal[:, :, None], diff, -jnp.inf))
        att = jnp.einsum('bhtk,bhtsk,bhsk->bhts', qc, decay, kc)
        o = o_inter + jnp.einsum('bhts,bhsv->bhtv', att, vc)
        b_last = b[:, :, -1:, :]
        state = jnp.exp(b_last[:, :, 0, :])[..., None] * state + jnp.einsum('bhsk,bhsv->bhkv', kc * jnp.exp(b_last - b), vc)
        return state, o

    s0 = jnp.zeros((bsz, B_HEADS, B_KEY_DIM, B_VAL_DIM), F32)
    _, o = lax.scan(step, s0, (qs, ks, vs, gs))
    o = o.transpose(1, 0, 3, 2, 4).reshape(bsz, seq, B_HEADS, B_VAL_DIM)
    o = rms_norm(o, norm_w.astype(F32).reshape(B_HEADS, B_VAL_DIM))
    return o.reshape(bsz, seq, B_V_W) * jax.nn.silu(g.astype(F32))

def ssd_chunked(xdt, adt, bm, cm):
    bsz, seq, h, p = xdt.shape
    nc = seq // CHUNK
    xc = xdt.reshape(bsz, nc, CHUNK, h, p)
    bc = bm.reshape(bsz, nc, CHUNK, h, C_STATE)
    cc = cm.reshape(bsz, nc, CHUNK, h, C_STATE)
    ac = adt.reshape(bsz, nc, CHUNK, h).transpose(0, 3, 1, 2)
    a_cum = jnp.cumsum(ac, axis=-1)
    lmat = jnp.exp(segsum(ac))
    y_diag = jnp.einsum('bclhn,bcshn,bhcls,bcshp->bclhp', cc, bc, lmat, xc)
    decay_states = jnp.exp(a_cum[..., -1:] - a_cum)
    states = jnp.einsum('bclhn,bhcl,bclhp->bchpn', bc, decay_states, xc)
    states = jnp.concatenate([jnp.zeros_like(states[:, :1]), states], axis=1)
    decay_chunk = jnp.exp(segsum(jnp.pad(a_cum[..., -1], ((0, 0), (0, 0), (1, 0)))))
    states = jnp.einsum('bhzc,bchpn->bzhpn', decay_chunk, states)[:, :-1]
    y_off = jnp.einsum('bclhn,bchpn,bhcl->bclhp', cc, states, jnp.exp(a_cum))
    return (y_diag + y_off).reshape(bsz, seq, h, p)

def mamba2_mixer(z, xbc, dt_raw, conv_w, conv_b, dt_bias, a_log, d_skip, norm_w):
    bsz, seq = z.shape[:2]
    conv = lax.conv_general_dilated(xbc.astype(F32), conv_w.astype(F32)[:, None, :], window_strides=(1,), padding=((C_CONV - 1, 0),), dimension_numbers=('NWC', 'WIO', 'NWC'), feature_group_count=C_CONV_DIM) + conv_b
    xbc = jax.nn.silu(conv)
    xs, bs, cs = jnp.split(xbc, [C_INNER, C_INNER + C_BC_W], axis=-1)
    rep = C_HEADS // C_GROUPS
    xs = xs.reshape(bsz, seq, C_HEADS, C_HEAD_DIM)
    bs = jnp.repeat(bs.reshape(bsz, seq, C_GROUPS, C_STATE), rep, axis=2)
    cs = jnp.repeat(cs.reshape(bsz, seq, C_GROUPS, C_STATE), rep, axis=2)
    dt = jax.nn.softplus(dt_raw.astype(F32) + dt_bias)
    a = -jnp.exp(a_log.astype(F32))
    y = ssd_chunked(xs * dt[..., None], a * dt, bs, cs)
    y = y + d_skip.astype(F32)[:, None] * xs
    y = y.reshape(bsz, seq, C_INNER) * jax.nn.silu(z.astype(F32))
    y = rms_norm(y.reshape(bsz, seq, C_GROUPS, C_INNER // C_GROUPS), norm_w.astype(F32).reshape(C_GROUPS, C_INNER // C_GROUPS))
    return y.reshape(bsz, seq, C_INNER)

def forgetting_attention(q, k, v, f_logit):
    bsz, seq = q.shape[:2]
    qh = q.astype(F32).transpose(0, 2, 1, 3)
    kh = k.astype(F32).transpose(0, 2, 1, 3)
    vh = v.astype(F32).transpose(0, 2, 1, 3)
    c = jnp.cumsum(jax.nn.log_sigmoid(f_logit.astype(F32)), axis=1).transpose(0, 2, 1)
    outs = []
    for blk in range(seq // D_QBLOCK):
        q0 = blk * D_QBLOCK
        q1 = q0 + D_QBLOCK
        s = jnp.einsum('bhqd,bhkd->bhqk', qh[:, :, q0:q1], kh[:, :, :q1]) * HEAD_DIM ** -0.5
        s = s + c[:, :, q0:q1, None] - c[:, :, None, :q1]
        causal = jnp.arange(q1)[None, :] <= (q0 + jnp.arange(D_QBLOCK))[:, None]
        p = jax.nn.softmax(jnp.where(causal, s, -jnp.inf), axis=-1)
        outs.append(jnp.einsum('bhqk,bhkd->bhqd', p, vh[:, :, :q1]))
    o = jnp.concatenate(outs, axis=2)
    return o.transpose(0, 2, 1, 3).reshape(bsz, seq, D_W)

def hybrid_mixer(h, w_in, a_sinks, rel_bias, lb, b_norm_w, c_conv_w, c_conv_b, c_dt_bias, c_a_log, c_d_skip, c_norm_w, d_f_bias, w_br_a, w_br_b, w_br_c, w_br_d, w_out):
    bsz, seq, _ = h.shape
    dt = h.dtype
    proj = h @ w_in
    cuts = [int(c) for c in np.cumsum(IN_SPLITS)[:-1]]
    (a_q, a_k, a_v, b_q, b_f, b_i, b_g, c_z, c_xbc, c_dt, d_q, d_k, d_v, d_f, gate) = jnp.split(proj, cuts, axis=-1)
    ya = swa_sink_attention(a_q.reshape(bsz, seq, A_HEADS, HEAD_DIM), a_k.reshape(bsz, seq, A_KV_HEADS, HEAD_DIM), a_v.reshape(bsz, seq, A_KV_HEADS, HEAD_DIM), a_sinks, t5_band_bias(rel_bias))
    yb = hgrn2_mixer(b_q, b_f, b_i, b_g, lb, b_norm_w)
    yc = mamba2_mixer(c_z, c_xbc, c_dt, c_conv_w, c_conv_b, c_dt_bias, c_a_log, c_d_skip, c_norm_w)
    yd = forgetting_attention(d_q.reshape(bsz, seq, D_HEADS, HEAD_DIM), d_k.reshape(bsz, seq, D_HEADS, HEAD_DIM), d_v.reshape(bsz, seq, D_HEADS, HEAD_DIM), d_f + d_f_bias)
    g = jax.nn.sigmoid(gate.astype(F32)).reshape(bsz, seq, N_BRANCH, D_MODEL)
    merged = (g[:, :, 0] * (ya.astype(dt) @ w_br_a) + g[:, :, 1] * (yb.astype(dt) @ w_br_b) + g[:, :, 2] * (yc.astype(dt) @ w_br_c) + g[:, :, 3] * (yd.astype(dt) @ w_br_d))
    return merged.astype(dt) @ w_out

def route(xf, w_router, router_bias):
    scores = jax.nn.sigmoid(xf @ w_router.astype(F32))
    sel = scores + router_bias.astype(F32)
    per_grp = N_EXPERTS // N_EXPERT_GROUPS
    grp_score = jnp.sum(lax.top_k(sel.reshape(-1, N_EXPERT_GROUPS, per_grp), 2)[0], axis=-1)
    _, top_grp = lax.top_k(grp_score, TOPK_GROUPS)
    grp_mask = jnp.any(top_grp[..., None] == jnp.arange(N_EXPERT_GROUPS), axis=1)
    sel = jnp.where(jnp.repeat(grp_mask, per_grp, axis=1), sel, -jnp.inf)
    _, idx = lax.top_k(sel, TOP_K)
    w = jnp.take_along_axis(scores, idx, axis=1)
    w = w / jnp.sum(w, axis=-1, keepdims=True) * ROUTED_SCALE
    return idx, w

def routed_experts(xf, idx, wts, wg, wu, wd):
    n_tok = xf.shape[0]
    n_asg = n_tok * TOP_K
    flat_e = idx.reshape(n_asg).astype(jnp.int32)
    flat_tok = jnp.arange(n_asg, dtype=jnp.int32) // TOP_K
    flat_w = wts.reshape(n_asg)
    order = jnp.argsort(flat_e)
    se = flat_e[order]
    counts = jnp.bincount(flat_e, length=N_EXPERTS).astype(jnp.int32)
    padded = (counts + MOE_BLOCK - 1) // MOE_BLOCK * MOE_BLOCK
    pad_end = jnp.cumsum(padded)
    pad_start = pad_end - padded
    grp_start = jnp.cumsum(counts) - counts
    dest = pad_start[se] + (jnp.arange(n_asg, dtype=jnp.int32) - grp_start[se])
    n_blocks = -(-n_asg // MOE_BLOCK) + N_EXPERTS
    n_steps = -(-n_blocks // MOE_BLOCKS_PER_STEP)
    n_rows = n_steps * MOE_BLOCKS_PER_STEP * MOE_BLOCK
    row_tok = jnp.zeros((n_rows,), jnp.int32).at[dest].set(flat_tok[order])
    row_w = jnp.zeros((n_rows,), F32).at[dest].set(flat_w[order])
    block_start = jnp.arange(n_steps * MOE_BLOCKS_PER_STEP, dtype=jnp.int32) * MOE_BLOCK
    block_e = jnp.minimum(jnp.searchsorted(pad_end, block_start, side='right'), N_EXPERTS - 1)
    row_tok = row_tok.reshape(n_steps, MOE_BLOCKS_PER_STEP, MOE_BLOCK)
    row_w = row_w.reshape(n_steps, MOE_BLOCKS_PER_STEP, MOE_BLOCK)
    block_e = block_e.reshape(n_steps, MOE_BLOCKS_PER_STEP)

    def step(acc, inp):
        tok, w, e = inp
        xb = xf[tok]
        hid = jax.nn.silu(jnp.einsum('nrd,ndf->nrf', xb, wg[e].astype(F32))) * jnp.einsum('nrd,ndf->nrf', xb, wu[e].astype(F32))
        yb = jnp.einsum('nrf,nfd->nrd', hid, wd[e].astype(F32)) * w[..., None]
        acc = acc.at[tok.reshape(-1)].add(yb.reshape(-1, D_MODEL))
        return acc, None

    acc, _ = lax.scan(step, jnp.zeros((n_tok, D_MODEL), F32), (row_tok, row_w, block_e))
    return acc

def moe_ffn(h, w_router, router_bias, wg, wu, wd, sg, su, sd):
    bsz, seq, d = h.shape
    xf = h.reshape(-1, d).astype(F32)
    idx, w = route(xf, w_router, router_bias)
    routed = routed_experts(xf, idx, w, wg, wu, wd)
    shared = (jax.nn.silu(xf @ sg.astype(F32)) * (xf @ su.astype(F32))) @ sd.astype(F32)
    return (routed + shared).reshape(bsz, seq, d).astype(h.dtype)

def setup_inputs(seed: int = 0) -> dict:
    key = jax.random.key(seed)
    ks = jax.random.split(key, 32)
    L = DEPTH

    def nrm(k, shape, scale):
        return jax.random.normal(k, shape, F32) * scale

    dt0 = jnp.exp(jax.random.uniform(ks[9], (L, C_HEADS), F32, np.log(1e-3), np.log(1e-1)))
    return {
        'x': nrm(ks[0], (BATCH, SEQ, D_MODEL), 1.0),
        'ln_in_g': 1.0 + nrm(ks[1], (D_MODEL,), 0.02),
        'ln_in_b': nrm(ks[2], (D_MODEL,), 0.02),
        'w_in': nrm(ks[3], (L, D_MODEL, D_IN), D_MODEL ** -0.5),
        'a_sinks': nrm(ks[4], (L, A_HEADS), 0.5),
        'rel_bias': nrm(ks[5], (REL_BUCKETS, A_HEADS), 0.5),
        'b_lower_bounds': nrm(ks[6], (L, B_K_W), 0.5),
        'b_norm_w': 1.0 + nrm(ks[7], (L, B_V_W), 0.02),
        'c_conv_w': nrm(ks[8], (L, C_CONV, C_CONV_DIM), C_CONV ** -0.5),
        'c_conv_b': nrm(ks[10], (L, C_CONV_DIM), 0.02),
        'c_dt_bias': dt0 + jnp.log(-jnp.expm1(-dt0)),
        'c_a_log': jnp.log(jax.random.uniform(ks[11], (L, C_HEADS), F32, 1.0, 16.0)),
        'c_d_skip': 1.0 + nrm(ks[12], (L, C_HEADS), 0.02),
        'c_norm_w': 1.0 + nrm(ks[13], (L, C_INNER), 0.02),
        'd_f_bias': jax.random.uniform(ks[14], (L, D_HEADS), F32, 1.0, 4.0),
        'w_br_a': nrm(ks[15], (L, A_Q_W, D_MODEL), A_Q_W ** -0.5),
        'w_br_b': nrm(ks[16], (L, B_V_W, D_MODEL), B_V_W ** -0.5),
        'w_br_c': nrm(ks[17], (L, C_INNER, D_MODEL), C_INNER ** -0.5),
        'w_br_d': nrm(ks[18], (L, D_W, D_MODEL), D_W ** -0.5),
        'w_out': nrm(ks[19], (L, D_MODEL, D_MODEL), D_MODEL ** -0.5 * DEEPNORM_BETA),
        'ln1_g': 1.0 + nrm(ks[20], (L, D_MODEL), 0.02),
        'ln1_b': nrm(ks[21], (L, D_MODEL), 0.02),
        'w_router': nrm(ks[22], (L, D_MODEL, N_EXPERTS), D_MODEL ** -0.5),
        'router_bias': nrm(ks[23], (L, N_EXPERTS), 0.01),
        'w_exp_gate': nrm(ks[24], (L, N_EXPERTS, D_MODEL, EXPERT_FF), D_MODEL ** -0.5),
        'w_exp_up': nrm(ks[25], (L, N_EXPERTS, D_MODEL, EXPERT_FF), D_MODEL ** -0.5),
        'w_exp_down': nrm(ks[26], (L, N_EXPERTS, EXPERT_FF, D_MODEL), EXPERT_FF ** -0.5 * DEEPNORM_BETA),
        'w_sh_gate': nrm(ks[27], (L, D_MODEL, SHARED_FF), D_MODEL ** -0.5),
        'w_sh_up': nrm(ks[28], (L, D_MODEL, SHARED_FF), D_MODEL ** -0.5),
        'w_sh_down': nrm(ks[29], (L, SHARED_FF, D_MODEL), SHARED_FF ** -0.5 * DEEPNORM_BETA),
        'ln2_g': 1.0 + nrm(ks[30], (L, D_MODEL), 0.02),
        'ln2_b': nrm(ks[31], (L, D_MODEL), 0.02),
    }

def reference(x, ln_in_g, ln_in_b, w_in, a_sinks, rel_bias, b_lower_bounds, b_norm_w, c_conv_w, c_conv_b, c_dt_bias, c_a_log, c_d_skip, c_norm_w, d_f_bias, w_br_a, w_br_b, w_br_c, w_br_d, w_out, ln1_g, ln1_b, w_router, router_bias, w_exp_gate, w_exp_up, w_exp_down, w_sh_gate, w_sh_up, w_sh_down, ln2_g, ln2_b):
    lower = jnp.cumsum(jax.nn.softmax(b_lower_bounds.astype(F32), axis=0), axis=0)
    lower = lower - lower[0]
    h = layer_norm(x, ln_in_g, ln_in_b)
    for l in range(DEPTH):
        mix = hybrid_mixer(h, w_in[l], a_sinks[l], rel_bias, lower[l], b_norm_w[l], c_conv_w[l], c_conv_b[l], c_dt_bias[l], c_a_log[l], c_d_skip[l], c_norm_w[l], d_f_bias[l], w_br_a[l], w_br_b[l], w_br_c[l], w_br_d[l], w_out[l])
        h = layer_norm(DEEPNORM_ALPHA * h + mix, ln1_g[l], ln1_b[l])
        ffn = moe_ffn(h, w_router[l], router_bias[l], w_exp_gate[l], w_exp_up[l], w_exp_down[l], w_sh_gate[l], w_sh_up[l], w_sh_down[l])
        h = layer_norm(DEEPNORM_ALPHA * h + ffn, ln2_g[l], ln2_b[l])
    return h


_drawn_inputs = setup_inputs


def setup_inputs(seed=0):
    import zlib

    import numpy as np

    out = dict(_drawn_inputs(seed))
    spreads = {}
    factors = {'a_sinks': 8.0, 'b_norm_w': 2.953, 'ln2_g': 2.766, 'ln2_b': 2.898}
    for name, (base, spread) in spreads.items():
        noise = np.random.default_rng([zlib.crc32(name.encode()), seed]).standard_normal(out[name].shape)
        drawn = base * np.exp(spread * noise) if base else spread * noise
        out[name] = jnp.asarray(drawn.astype(out[name].dtype))
    for name, factor in factors.items():
        out[name] = (out[name] * factor).astype(out[name].dtype)
    return out
```

```python
from contextlib import ExitStack

import numpy as np
import concourse.bass as bass
from concourse import mybir

F32 = mybir.dt.float32
BF16 = mybir.dt.bfloat16
U32 = mybir.dt.uint32
I32 = mybir.dt.int32
ALU = mybir.AluOpType
ACT = mybir.ActivationFunctionType
AX = mybir.AxisListType

P = 128
D = 1024
T = 1024
KT = D // P
NT = T // P
HALF = 512
HD = 64
A_HEADS, A_PAIRS = 8, 4
WIN = 192
SUB = 16
NSUB = P // SUB
NE, TOPK, GROUPS, TOPG = 64, 6, 8, 4
FF = 256
OVER = 47
ALPHA = 2.0 ** 0.25
ROUTED_SCALE = 2.5
LN_EPS, RMS_EPS = 1e-5, 1e-6
NEG = -1e30
GATES_A, GATES_B, GATES_C, GATES_D = 2, 2, 3, 5
SPILLED = GATES_A + GATES_B + GATES_C + GATES_D
CLAMP = 80.0

AQ, AK, AV, BQ, BF, BI, BG, CZ, CX, CB = 0, 512, 640, 768, 1024, 1280, 1536, 1792, 2048, 2304
CDT, DQ, DK, DV, DF, GATE = 2560, 2564, 2820, 3076, 3332, 3336

HT0 = 0
YT0 = HT0 + KT * T
W0 = YT0 + 10 * T
SLOT = KT * 256
R1 = W0 + 2 * SLOT
R2 = R1 + 8192
R3 = R2 + 8192
WK = R3 + 6400
ARENA = WK + 5400


class Shared:
    pass


class Slot:

    def __init__(self, pieces, units):
        self.pieces, self.units = pieces, units


def bcast(ap, shape):
    return ap.to_broadcast(shape)


def setup(nc, ctx, ins):
    g = Shared()
    g.nc, g.ctx, g.ins = nc, ctx, ins

    def sb(name, shape, dt=F32):
        return ctx.enter_context(nc.sbuf_tensor(name, shape, dt))

    stage_sems = []

    def keep(name):
        return nc.alloc_semaphore(name=name)

    def sem(name):
        stage_sems.append(keep(name))
        return stage_sems[-1]

    def release():
        nc.clear_and_free_semaphores(stage_sems)
        stage_sems.clear()
        nc.all_engine_barrier()

    g.sb, g.sem, g.keep, g.release = sb, sem, keep, release
    g.arena = sb("arena", [P, ARENA])

    def region(at, *dims):
        n = int(np.prod(dims))
        assert at + n <= ARENA
        names = "abcd"[:len(dims)]
        ap = g.arena[:, at:at + n]
        if len(dims) == 1:
            return ap
        kw = {c: d for c, d in zip(names, dims)}
        return ap.rearrange(f"p ({' '.join(names)}) -> p {' '.join(names)}", **kw)

    g.region = region
    g.bank = ctx.enter_context(nc.psum_tensor("banks", [P, 8, HALF], F32))
    g.hT = region(HT0, KT, T)
    g.yT = region(YT0, 10, T)
    g.wslot = [region(W0 + i * SLOT, KT, 256) for i in range(2)]

    g.qA = region(R1, A_PAIRS, T)
    g.kA = region(R1 + 4096, 2, HD + T)
    g.vA = region(R1 + 4096 + 2 * (HD + T), NT, P)
    g.qB = region(R2, 2, T)
    g.fB = region(R2 + 2048, 2, T)
    g.igB = region(R2 + 4096, NT, 512)
    g.cX = region(R3, 4, T + 3)
    g.zC = region(R3 + 4 * (T + 3), NT, 256)
    g.qD = region(R1, 2, T)
    g.kD = region(R1 + 2048, 2, 2, T)
    g.vD = region(R1 + 2048 + 4096, NT, 256)

    g.ident = sb("ident", [P, P])
    g.neg_below = sb("neg_below", [P, P])
    g.neg_above = sb("neg_above", [P, P])
    g.g_in, g.b_in = sb("g_in", [P, KT]), sb("b_in", [P, KT])
    g.rows = sb("rows", [8, T])
    g.sinks = sb("sinks", [P, A_HEADS])
    g.dskip = sb("dskip", [P, 4])
    g.rowbias, g.rowlog = sb("rowbias", [8, 1]), sb("rowlog", [8, 1])
    g.lbB = sb("lbB", [P, 2])
    g.normB, g.normC = sb("normB", [P, 2]), sb("normC", [P, 2])
    g.convw, g.convb = sb("convw", [P, 4, 4]), sb("convb", [P, 4])
    g.relb, g.onehot = sb("relb", [32, A_HEADS]), region(YT0 + 9 * T, 256)[0:32]
    g.index, g.list, g.flag = sb("index", [P, 4, 2], U32), sb("list", [P, 4, 3]), sb("flag", [P, 2])
    g.relwide = region(WK + 3584, A_HEADS, P)[0:32]
    g.const_ready, g.params = keep("const_ready"), keep("params")
    g.proj_ready, g.proj_read = keep("proj_ready"), keep("proj_read")
    g.w_loaded = [keep("w_loaded0"), keep("w_loaded1")]
    return g



def plan_slots(g):
    w = g.ins["w_in"][0].rearrange("(k p) n -> p k n", p=P)
    S = []

    def slot(pieces, units):
        S.append(Slot(pieces=[(at, w[:, :, c:c + n]) for at, c, n in pieces], units=units))

    def whole(c):
        return [(0, c, 256)]

    def fm(dst, col=0, width=P):
        return [("fm", col, width, h, dst) for h in range(2)]

    def tm(dst, col, width, per):
        return [("tm", col, width, m, dst) for m in range(0, NT, per)]

    def plain(dst):
        return lambda act, h, bank: [(dst[:, h * HALF:(h + 1) * HALF], bank)]

    def halves(dst, off):
        return lambda act, h, bank: [
            (dst[0:HD, 0, off + h * HALF:off + (h + 1) * HALF], bank[0:HD]),
            (dst[HD:P, 1, off + h * HALF:off + (h + 1) * HALF], bank[HD:P])]

    slot([(0, CDT, 4), (4, DF, 4)], fm(lambda act, h, bank: [(g.rows[:, h * HALF:(h + 1) * HALF], bank)], 0, 8))
    slot([(64 * i, AQ + 64 * c, 64) for i, c in enumerate((0, 4, 1, 5))],
         fm(plain(g.qA[:, 0, :])) + fm(plain(g.qA[:, 1, :]), P))
    slot([(64 * i, AQ + 64 * c, 64) for i, c in enumerate((2, 6, 3, 7))],
         fm(plain(g.qA[:, 2, :])) + fm(plain(g.qA[:, 3, :]), P))
    slot(whole(AK), fm(halves(g.kA, HD)) + tm(
        lambda act, m, bank: [(g.vA[:, m:m + 4, :], bank.rearrange("p (m n) -> p m n", m=4))], P, P, 4))

    def wide(dst, c):
        return lambda act, m, bank: [(dst[:, m:m + 2, c:c + 256], bank.rearrange("p (m n) -> p m n", m=2))]

    slot(whole(BF), fm(plain(g.fB[:, 0, :])) + fm(plain(g.fB[:, 1, :]), P))
    slot(whole(BQ), fm(plain(g.qB[:, 0, :])) + fm(plain(g.qB[:, 1, :]), P))
    slot(whole(BI), tm(wide(g.igB, 0), 0, 256, 2))
    slot(whole(BG), tm(wide(g.igB, 256), 0, 256, 2))
    for c in range(2):
        slot(whole(CX + 256 * c), fm(plain(g.cX[:, 2 * c, 3:3 + T])) + fm(plain(g.cX[:, 2 * c + 1, 3:3 + T]), P))
    slot(whole(CZ), tm(wide(g.zC, 0), 0, 256, 2))
    g.S = S
    g.slots_a = len(S)
    gate_slots(g, 0, GATES_A)
    g.slots_b = len(S)
    slot(whole(DQ), fm(plain(g.qD[:, 0, :])) + fm(plain(g.qD[:, 1, :]), P))
    slot(whole(DK), fm(halves(g.kD[:, 0], 0)) + fm(halves(g.kD[:, 1], 0), P))
    slot(whole(DV), tm(wide(g.vD, 0), 0, 256, 2))
    gate_slots(g, GATES_A, GATES_A + GATES_B)
    g.slots_c = len(S)
    gate_slots(g, GATES_A + GATES_B, GATES_A + GATES_B + GATES_C)
    g.slots_d = len(S)
    gate_slots(g, GATES_A + GATES_B + GATES_C, SPILLED)
    g.slots_merge = len(S)
    gate_slots(g, SPILLED, KT // 2 * 4)
    g.U = [(n, u) for n, s in enumerate(S) for u in s.units]
    g.first_unit = [sum(len(s.units) for s in S[:n]) for n in range(len(S) + 1)]
    g.gate_unit = [u for u, (n, unit) in enumerate(g.U) if unit[4] is None]
    g.gate_number = {u: v for v, u in enumerate(g.gate_unit)}
    g.gates = g.nc.dram_tensor("gates", [4 * SPILLED, P, HALF], F32, kind="Internal").ap()
    g.spilled = g.keep("spilled")


def gate_slots(g, first, last):
    w = g.ins["w_in"][0].rearrange("(k p) n -> p k n", p=P)
    for q in range(first, last):
        jj, b = divmod(q, 4)
        c = GATE + b * D + jj * 256
        g.S.append(Slot(pieces=[(0, w[:, :, c:c + 256])],
                        units=[("fm", i * P, P, h, None) for i in range(2) for h in range(2)]))


def load_slot(g, sp, n):
    if n >= 2:
        sp.wait_ge(g.proj_ready, g.first_unit[n - 1])
    for at, src in g.S[n].pieces:
        sp.dma_start(g.wslot[n % 2][:, :, at:at + src.shape[2]], src).then_inc(g.w_loaded[n % 2], 16)


def slot_bytes(g, n):
    return 16 * sum(len(s.pieces) for s in g.S[n % 2:n + 1:2])


def proj_bank(g, u, banks):
    return g.bank[:, banks[u % len(banks)], :]


def project_unit(g, pe, u, banks):
    for q in range(KT):
        project_part(g, pe, u, q, banks)


def project_part(g, pe, u, q, banks):
    n, (kind, col, width, at, _) = g.U[u]
    if u == g.first_unit[n] and q == 0:
        pe.wait_ge(g.w_loaded[n % 2], slot_bytes(g, n))
    if u >= len(banks) and q == 0:
        pe.wait_ge(g.proj_read, u - len(banks) + 1)
    w, bank = g.wslot[n % 2], proj_bank(g, u, banks)
    if kind == "fm":
        mm = pe.matmul(bank[0:width], w[:, q, col:col + width], g.hT[:, q, at * HALF:(at + 1) * HALF],
                       start=(q == 0), stop=(q == KT - 1))
    else:
        per = HALF // width
        for i in range(q * per, (q + 1) * per):
            m, k = divmod(i, KT)
            mm = pe.matmul(bank[:, m * width:(m + 1) * width],
                           g.hT[:, k, (at + m) * P:(at + m + 1) * P], w[:, k, col:col + width],
                           start=(k == 0), stop=(k == KT - 1))
    if q == KT - 1:
        mm.then_inc(g.proj_ready, 1)


def read_unit(g, act, u, banks):
    n, (kind, col, width, at, place) = g.U[u]
    act.wait_ge(g.proj_ready, u + 1)
    bank = proj_bank(g, u, banks)
    for dst, src in place(act, at, bank if kind == "tm" else bank[0:width]):
        ins = act.activation(dst, src, ACT.Copy)
    ins.then_inc(g.proj_read, 1)



def filler(g, pe, first_slot, last_slot):
    parts = [(u, q) for u in range(g.first_unit[first_slot], g.first_unit[last_slot]) for q in range(KT)]

    def fill(n=None):
        n = len(parts) if n is None else n
        for u, q in parts[:n]:
            project_part(g, pe, u, q, (6, 7))
        del parts[:n]

    return fill


def stage_gate(g, act, u, staging):
    v = g.gate_number[u]
    act.wait_ge(g.proj_ready, u + 1)
    if v:
        act.wait_ge(g.spilled, 16 * v)
    act.activation(staging, proj_bank(g, u, (6, 7)), ACT.Copy).then_inc(g.proj_read, 1)


def stager(g, act, first_slot, last_slot, staging):
    units = list(range(g.first_unit[first_slot], g.first_unit[last_slot]))
    done = [0]

    def stage(n=None):
        n = len(units) if n is None else min(n, len(units))
        for u in units[done[0]:n]:
            stage_gate(g, act, u, staging)
        done[0] = max(done[0], n)

    return stage


def spill_gates(g, sp, first_slot, last_slot, staging):
    for n in range(first_slot, last_slot):
        for u in range(g.first_unit[n], g.first_unit[n + 1]):
            if u in g.gate_number:
                sp.wait_ge(g.proj_read, u + 1)
                v = g.gate_number[u]
                sp.dma_start(g.gates[v], staging).then_inc(g.spilled, 16)
        load_slot(g, sp, n + 2)
    sp.wait_ge(g.spilled, 16 * (v + 1))

def norm_in(g):
    nc, sem, bank = g.nc, g.sem, g.bank
    x = g.region(YT0, NT, D)
    stats, mv = g.sb("stats0", [P, NT, 2, 6]), g.sb("mv0", [P, NT, 2])
    rstd = g.sb("rstd0", [P, NT])
    relval = g.region(WK + A_HEADS * WIN, A_HEADS, 256)
    skew = nc.dram_tensor("skew", [P * A_HEADS * 256], F32, kind="Internal").ap()
    g.biasA = g.region(WK, A_HEADS, WIN)
    stat_done, mean_done, var_eps, std_done, rstd_done = map(sem, (
        "stat_done", "mean_done", "var_eps", "std_done", "rstd_done"))
    x_in = [sem(f"x_in{m}") for m in range(NT)]
    x_normed, xT_ready, xT_read = sem("x_normed"), sem("xT_ready"), [sem("xT_read0"), sem("xT_read1")]
    zeroed, rel_wide, rel_ready, rel_read, rel_stored, bias_in = map(sem, (
        "zeroed", "rel_wide", "rel_ready", "rel_read", "rel_stored", "bias_in"))
    xt = g.ins["x"][0].rearrange("(m p) d -> m p d", p=P)

    with nc.Block() as block:
        @block.sync
        def _(sp):
            for m in range(NT):
                sp.dma_start(x[:, m, :], xt[m]).then_inc(x_in[m], 16)
            load_slot(g, sp, 0)
            load_slot(g, sp, 1)
            sp.wait_ge(rel_read, 4)
            sp.dma_start(skew.rearrange("(p n) -> p n", p=P),
                         relval.rearrange("p a b -> p (a b)")).then_inc(rel_stored, 16)
            sp.wait_ge(rel_stored, 16)
            wide = A_HEADS * 256
            view = bass.AP(tensor=skew.tensor, offset=63, ap=[[wide - 1, P], [256, A_HEADS], [1, WIN]])
            sp.dma_start(g.biasA, view).then_inc(bias_in, 16)
            sp.wait_ge(bias_in, 16)

        @block.gpsimd
        def _(pool):
            pool.memset(g.ident[:], 0.0).then_inc(zeroed, 1)
            pool.memset(g.neg_below[:], 0.0).then_inc(zeroed, 1)
            pool.memset(g.neg_above[:], 0.0).then_inc(zeroed, 1)
            pool.wait_ge(zeroed, 3)
            pool.affine_select(out=g.ident[:], in_=g.ident[:], compare_op=ALU.not_equal, fill=1.0, base=0,
                               pattern=[[-1, P]], channel_multiplier=1).then_inc(g.const_ready, 1)
            pool.affine_select(out=g.neg_below[:], in_=g.neg_below[:], compare_op=ALU.is_ge, fill=NEG, base=0,
                               pattern=[[1, P]], channel_multiplier=-1).then_inc(g.const_ready, 1)
            pool.affine_select(out=g.neg_above[:], in_=g.neg_above[:], compare_op=ALU.is_ge, fill=NEG, base=0,
                               pattern=[[-1, P]], channel_multiplier=1).then_inc(g.const_ready, 1)

        @block.scalar
        def _(act):
            def row(a):
                return a.rearrange("(a n) -> a n", a=1)

            def col(a, n):
                return a.rearrange("(k p) -> p k", k=n)

            loads = [
                (g.relb[:], g.ins["rel_bias"]), (g.onehot, g.ins["bucket_onehot"]),
                (g.g_in[:], col(g.ins["ln_in_g"], KT)), (g.b_in[:], col(g.ins["ln_in_b"], KT)),
                (g.sinks[:], row(g.ins["a_sinks"][0]).to_broadcast([P, A_HEADS])),
                (g.dskip[:], row(g.ins["c_d_skip"][0]).to_broadcast([P, 4])),
                (g.rowbias[0:4], col(g.ins["c_dt_bias"][0], 1)), (g.rowbias[4:8], col(g.ins["d_f_bias"][0], 1)),
                (g.rowlog[0:4], col(g.ins["c_a_log"][0], 1)), (g.rowlog[4:8], g.ins["zero4"].rearrange("(p a) -> p a", a=1)),
                (g.lbB[:], col(g.ins["b_lower_bounds"][0], 2)),
                (g.normB[:], col(g.ins["b_norm_w"][0], 2)), (g.normC[:], col(g.ins["c_norm_w"][0], 2)),
                (g.convb[:], col(g.ins["c_conv_b"][0], 4))]
            for dst, src in loads:
                act.dma_start(dst, src, allow_slow_non_contiguous=True).then_inc(g.params, 16)
            for i in range(4):
                act.dma_start(g.convw[:, :, i], col(g.ins["c_conv_w"][0, i], 4), allow_slow_non_contiguous=True).then_inc(g.params, 16)
            g.n_params = 16 * (len(loads) + 4)
            for i in range(4):
                act.wait_ge(rel_ready, i + 1)
                act.activation(relval[:, 2 * i:2 * i + 2, :],
                               bank[:, 4 + i, :].rearrange("p (h n) -> p h n", h=2),
                               ACT.Copy, scale=8.0).then_inc(rel_read, 1)
            act.wait_ge(var_eps, 1)
            act.activation(rstd[:], rstd[:], ACT.Sqrt).then_inc(std_done, 1)
            for h in range(2):
                for k in range(0, KT, 2):
                    i = h * KT + k
                    act.wait_ge(xT_ready, i + 1)
                    act.activation(g.hT[:, k, h * HALF:(h + 1) * HALF], bank[:, i % 4, :], ACT.Identity,
                                   bias=g.b_in[:, k:k + 1], scale=g.g_in[:, k:k + 1]).then_inc(xT_read[0], 1)

        @block.vector
        def _(dve):
            dve.wait_ge(g.params, g.n_params)
            dve.tensor_copy(g.relwide, bcast(g.relb[:].unsqueeze(2), [32, A_HEADS, P])).then_inc(rel_wide, 1)
            for m in range(NT):
                dve.wait_ge(x_in[m], 16)
                for i in range(2):
                    dve.bn_stats(stats[:, m, i, :], x[:, m, i * HALF:(i + 1) * HALF]).then_inc(stat_done, 1)
            for m in range(NT):
                dve.wait_ge(stat_done, 2 * (m + 1))
                dve.bn_aggr(mv[:, m, :], stats[:, m]).then_inc(mean_done, 1)
            dve.wait_ge(mean_done, NT)
            dve.tensor_scalar(rstd[:], mv[:, :, 1], LN_EPS, None, ALU.add).then_inc(var_eps, 1)
            dve.wait_ge(std_done, 1)
            dve.reciprocal(rstd[:], rstd[:]).then_inc(rstd_done, 1)
            dve.wait_ge(rstd_done, 1)
            for m in range(NT):
                dve.tensor_scalar(x[:, m, :], x[:, m, :], mv[:, m, 0:1], rstd[:, m:m + 1],
                                  ALU.subtract, ALU.mult).then_inc(x_normed, 1)
            for h in range(2):
                for k in range(1, KT, 2):
                    i = h * KT + k
                    dve.wait_ge(xT_ready, i + 1)
                    dve.tensor_scalar(g.hT[:, k, h * HALF:(h + 1) * HALF], bank[:, i % 4, :],
                                      g.g_in[:, k:k + 1], g.b_in[:, k:k + 1],
                                      ALU.mult, ALU.add).then_inc(xT_read[1], 1)

        @block.tensor
        def _(pe):
            pe.wait_ge(rel_wide, 1)
            for h in range(A_HEADS):
                mm = pe.matmul(bank[:, 4 + h // 2, (h % 2) * 256:(h % 2 + 1) * 256],
                               g.relwide[:, h, :], g.onehot, start=True, stop=True)
                if h % 2:
                    mm.then_inc(rel_ready, 1)
            pe.wait_ge(g.const_ready, 3)
            for h in range(2):
                pe.wait_ge(x_normed, 4 * (h + 1))
                for k in range(KT):
                    i = h * KT + k
                    if i >= 4:
                        pe.wait_ge(xT_read[i % 2], (i - 4) // 2 + 1)
                    for m in range(4):
                        mm = pe.transpose(bank[:, i % 4, m * P:(m + 1) * P],
                                          x[:, 4 * h + m, k * P:(k + 1) * P], g.ident[:])
                    mm.then_inc(xT_ready, 1)



def project(g):
    banks = (6, 7)
    n_units = g.first_unit[g.slots_a]
    g.banks = banks
    zero_pad = g.sem("zero_pad")
    with g.nc.Block() as block:
        @block.sync
        def _(sp):
            for n in range(2, g.slots_a + 2):
                load_slot(g, sp, n)

        @block.gpsimd
        def _(pool):
            pool.memset(g.kA[:, :, 0:HD], 0.0).then_inc(zero_pad, 1)
            pool.memset(g.cX[:, :, 0:3], 0.0).then_inc(zero_pad, 1)
            pool.wait_ge(zero_pad, 2)
            pool.memset(g.kA[HD:P, 0, HD:], 0.0).then_inc(zero_pad, 1)
            pool.wait_ge(zero_pad, 3)
            pool.memset(g.kA[0:HD, 1, HD:], 0.0).then_inc(zero_pad, 1)

        @block.tensor
        def _(pe):
            for u in range(n_units):
                project_unit(g, pe, u, banks)

        @block.scalar
        def _(act):
            for u in range(n_units):
                read_unit(g, act, u, banks)



def mix_a(g):
    nc, sem, bank = g.nc, g.sem, g.bank
    probs = [g.region(WK + 1536 + 512 * i, 2, 256) for i in range(2)]
    probsT = [g.region(WK + 2560 + 512 * i, 2, 2, P) for i in range(2)]
    y = g.region(WK + 3584, A_HEADS * HD)
    maxA, negA = g.sb("maxA", [P, NT, 2, 4]), g.sb("negA", [P, NT, 2, 4])
    sumA, sinkA = g.sb("sumA", [P, NT, 2, 4]), g.sb("sinkA", [P, NT, 2, 4])
    N = NT * 4
    staging = g.region(WK + 4864, HALF)
    (scores, rowmax, negmax, probs_done, pT_ready, pT_read, pv_done, sink_gap, sink_exp, den_done, rden,
     y_done, yT_ready, yT_read, masked) = [sem("a_" + n) for n in (
         "scores", "rowmax", "negmax", "probs", "pT_ready", "pT_read", "pv", "sink_gap", "sink_exp", "den",
         "rden", "y", "yT_ready", "yT_read", "masked")]

    def lo(m):
        return HD if m == 0 else 0

    def read_yT(act, m):
        act.wait_ge(yT_ready, m + 1)
        act.activation(g.yT[:, 0:4, m * P:(m + 1) * P], bank[:, 5, :].rearrange("p (c n) -> p c n", c=4),
                       ACT.Copy).then_inc(yT_read, 1)

    with nc.Block() as block:
        @block.sync
        def _(sp):
            spill_gates(g, sp, g.slots_a, g.slots_b, staging)

        @block.gpsimd
        def _(pool):
            for b in range(2):
                pool.memset(probs[b], 0.0).then_inc(masked, 1)
            pool.wait_ge(masked, 2)
            pool.memset(g.biasA[0:HD, :, P:WIN], 8 * NEG).then_inc(masked, 1)
            pool.wait_ge(masked, 3)
            pool.memset(g.biasA[HD:P, :, 0:HD], 8 * NEG).then_inc(masked, 1)

        @block.tensor
        def _(pe):
            def score(u):
                m, j = divmod(u, 4)
                if u >= 2:
                    pe.wait_ge(rowmax, 2 * (u - 1))
                pe.matmul(bank[:, u % 2, 0:2 * WIN], g.qA[:, j, m * P:(m + 1) * P],
                          g.kA[:, :, m * P:m * P + WIN], start=True, stop=True).then_inc(scores, 1)

            def turn(u):
                pe.wait_ge(probs_done, 2 * (u + 1))
                if u >= 2:
                    pe.wait_ge(pT_read, u - 1)
                for h in range(2):
                    for c in range(2):
                        mm = pe.transpose(bank[:, 2 + u % 2, (2 * h + c) * P:(2 * h + c + 1) * P],
                                          probs[u % 2][:, h, c * P:(c + 1) * P], g.ident[:])
                mm.then_inc(pT_ready, 1)

            def values(u):
                m, j = divmod(u, 4)
                pe.wait_ge(pT_read, u + 1)
                if j == 0 and m >= 1:
                    pe.wait_ge(y_done, m)
                for h in range(2):
                    out = bank[:, 4, (4 * h + j) * HD:(4 * h + j + 1) * HD]
                    if m:
                        pe.matmul(out, probsT[u % 2][:, h, 0, :], g.vA[:, m - 1, h * HD:(h + 1) * HD],
                                  start=True, stop=False)
                    mm = pe.matmul(out, probsT[u % 2][:, h, 1, :], g.vA[:, m, h * HD:(h + 1) * HD],
                                   start=(m == 0), stop=True)
                mm.then_inc(pv_done, 1)

            def turn_y(m):
                pe.wait_ge(y_done, m + 1)
                if m:
                    pe.wait_ge(yT_read, m)
                for c in range(4):
                    mm = pe.transpose(bank[:, 5, c * P:(c + 1) * P], y[:, c * P:(c + 1) * P], g.ident[:])
                mm.then_inc(yT_ready, 1)

            fill = filler(g, pe, g.slots_a, g.slots_b)
            pe.wait_ge(masked, 4)
            for i in range(N + 5):
                if i < N:
                    score(i)
                fill(1)
                if 2 <= i < N + 2:
                    turn(i - 2)
                fill(1)
                if 3 <= i < N + 3:
                    values(i - 3)
                if i >= 8 and (i - 8) % 4 == 0:
                    turn_y((i - 8) // 4)
            fill()

        @block.vector
        def _(dve):
            dve.wait_ge(masked, 4)

            def row_max(u):
                m, j = divmod(u, 4)
                dve.wait_ge(scores, u + 1)
                if u >= 2:
                    dve.wait_ge(pT_ready, u - 1)
                s = bank[:, u % 2, 0:2 * WIN].rearrange("p (h n) -> p h n", h=2)
                for h in range(2):
                    dve.tensor_tensor_reduce(
                        out=probs[u % 2][:, h, HD + lo(m):], in0=s[:, h, lo(m):],
                        in1=g.biasA[:, 4 * h + j, lo(m):], scale=0.125, scalar=g.sinks[:, 4 * h + j:4 * h + j + 1],
                        op0=ALU.add, op1=ALU.max, accum_out=maxA[:, m, h, j:j + 1]).then_inc(rowmax, 1)
                dve.wait_ge(rowmax, 2 * (u + 1))
                dve.tensor_scalar(negA[:, m, :, j], maxA[:, m, :, j], -1.0, None, ALU.mult).then_inc(negmax, 1)

            def turned(u):
                dve.wait_ge(pT_ready, u + 1)
                if u >= 2:
                    dve.wait_ge(pv_done, u - 1)
                dve.tensor_copy(probsT[u % 2].rearrange("p a b n -> p (a b n)"),
                                bank[:, 2 + u % 2, :]).then_inc(pT_read, 1)

            def norm(m):
                dve.wait_ge(sink_exp, m + 1)
                dve.tensor_tensor(sumA[:, m], sumA[:, m], sinkA[:, m], ALU.add).then_inc(den_done, 1)
                dve.wait_ge(den_done, m + 1)
                dve.reciprocal(sumA[:, m], sumA[:, m]).then_inc(rden, 1)
                dve.wait_ge(rden, m + 1)
                dve.wait_ge(pv_done, 4 * (m + 1))
                if m:
                    dve.wait_ge(yT_ready, m)
                dve.tensor_tensor(y.rearrange("p (h n) -> p h n", h=A_HEADS),
                                  bank[:, 4, :].rearrange("p (h n) -> p h n", h=A_HEADS),
                                  bcast(sumA[:, m].rearrange("p a b -> p (a b)").unsqueeze(2), [P, A_HEADS, HD]),
                                  ALU.mult).then_inc(y_done, 1)

            for i in range(N + 4):
                if i < N:
                    row_max(i)
                    if i % 4 == 3:
                        m = i // 4
                        dve.wait_ge(negmax, i + 1)
                        dve.tensor_tensor(sinkA[:, m].rearrange("p a b -> p (a b)"), g.sinks[:],
                                          negA[:, m].rearrange("p a b -> p (a b)"), ALU.add).then_inc(sink_gap, 1)
                if 2 <= i < N + 2:
                    turned(i - 2)
                if i >= 7 and (i - 7) % 4 == 0:
                    norm((i - 7) // 4)

        @block.scalar
        def _(act):
            stage = stager(g, act, g.slots_a, g.slots_b, staging)
            for u in range(N + 1):
                if u < N:
                    m, j = divmod(u, 4)
                    act.wait_ge(negmax, u + 1)
                    for h in range(2):
                        p = probs[u % 2][:, h, HD + lo(m):]
                        act.activation(p, p, ACT.Exp, bias=negA[:, m, h, j:j + 1],
                                       accum_out=sumA[:, m, h, j:j + 1]).then_inc(probs_done, 1)
                    if j == 3:
                        act.wait_ge(sink_gap, m + 1)
                        act.activation(sinkA[:, m], sinkA[:, m], ACT.Exp).then_inc(sink_exp, 1)
                stage(2 * u // KT)
                if u >= 9 and (u - 9) % 4 == 0:
                    m = (u - 9) // 4
                    read_yT(act, m)
            for m in range(NT - 2, NT):
                read_yT(act, m)
            stage()



def mix_b(g):
    nc, sem, bank = g.nc, g.sem, g.bank
    N = 2 * NT
    key = g.region(YT0 + 6144, 2, T)
    gapsb = [g.region(YT0 + 8192 + 1024 * i, NSUB, P) for i in range(2)]
    o_all = g.region(WK, NT, 256)
    at = WK + 2048
    ones_rows = g.region(at, T)
    qz = [g.region(at + 1024 + 256 * i, 2, P) for i in range(2)]
    att = [g.region(at + 1536 + 256 * i, 2, P) for i in range(2)]
    expb = g.region(at + 2048, P)
    qdec = g.region(at + 2176, P)
    kdec = g.region(at + 2304, P)
    kdecT = g.region(at + 2432, P)
    state = g.region(at + 2560, 2, 2, HD)
    qgap = g.region(at + 2816, NSUB, SUB)
    sq = g.region(YT0 + 8192, NT, 256)
    lb, oml = g.sb("lb", [P, 2]), g.sb("oml", [P, 2])
    ss = g.sb("ssB", [P, NT, 4])
    zeroed = g.sem("zero_kd")
    (lb0, lb1, lb2, lb3, sig, gate, keyed, floored, logged, scanned, cleared, gap, gap_min, gap_exp, kf, qg, qg_min,
     qg_exp, qz_done, expb_done, qdec_done, klast, kdec_done, att_ready, att_read, att_cut, kT_ready, kT_read, o_ready,
     o_read, u_ready, st_done, gt, silu1, silu2, sqd, ssd, sse, ssq, ssr, n1, n2, yT_ready, yT_read) = [
        sem("b_" + n) for n in (
            "lb0 lb1 lb2 lb3 sig gate keyed floored logged scanned cleared gap gap_min gap_exp kf qg qg_min "
            "qg_exp qz expb qdec klast kdec att_ready att_read att_cut kT_ready kT_read o_ready "
            "o_read u_ready state gt silu1 silu2 sq ss sse ssq ssr n1 n2 yT_ready yT_read").split()]
    g_in = g.igB[:, :, 256:512]
    f_all = g.region(R2 + 2048, 2048)
    key_all = g.region(YT0 + 6144, 2048)
    gt_buf = g.region(YT0 + 6144, NT, 256)

    staging = ones_rows[:, 0:HALF]
    gates_from = g.first_unit[g.slots_c - GATES_B]
    beside = list(range(g.first_unit[g.slots_b], g.first_unit[g.slots_c]))

    def tile(ap, m):
        return ap[:, m * P:(m + 1) * P]

    def mids(j, m):
        return g.fB[:, j, m * P + SUB // 2 - 1:(m + 1) * P:SUB]

    def cut(pool, u):
        pool.wait_ge(att_read, u + 1)
        pool.affine_select(out=att[u % 2], in_=att[u % 2], compare_op=ALU.is_ge, fill=0.0, base=0,
                           pattern=[[0, 2], [1, P]], channel_multiplier=-1).then_inc(att_cut, 1)

    with nc.Block() as block:
        @block.sync
        def _(sp):
            spill_gates(g, sp, g.slots_b, g.slots_c, staging)

        @block.gpsimd
        def _(pool):
            pool.memset(g.kD[HD:P, :, 0, :], 0.0).then_inc(zeroed, 1)
            pool.wait_ge(zeroed, 1)
            pool.memset(g.kD[0:HD, :, 1, :], 0.0).then_inc(zeroed, 1)
            pool.wait_ge(zeroed, 2)
            pool.memset(ones_rows, 1.0).then_inc(cleared, 1)
            pool.wait_ge(cleared, 1)
            pool.memset(ones_rows[:, 0:T:P], 0.0).then_inc(cleared, 1)
            for i in range(2):
                pool.memset(qz[i], 0.0).then_inc(cleared, 1)
            pool.memset(state, 0.0).then_inc(cleared, 1)
            for u in range(N):
                m, j = divmod(u, 2)
                b = tile(g.fB[:, j, :], m)
                pool.wait_ge(scanned, 2)
                if u >= 2:
                    pool.wait_ge(att_ready, u - 1)
                pool.tensor_tensor(gapsb[u % 2], bcast(mids(j, m).unsqueeze(2), [P, NSUB, P]),
                                   bcast(b.unsqueeze(1), [P, NSUB, P]), ALU.subtract).then_inc(gap, 1)
                if u >= 1:
                    cut(pool, u - 1)
            cut(pool, N - 1)

        @block.scalar
        def _(act):
            def read_beside(n=1):
                for u in beside[:n]:
                    if u < gates_from:
                        read_unit(g, act, u, (6, 7))
                    else:
                        stage_gate(g, act, u, staging)
                del beside[:n]

            act.activation(f_all, f_all, ACT.Sigmoid).then_inc(sig, 1)
            act.wait_ge(lb0, 1)
            act.activation(lb[:], lb[:], ACT.Exp).then_inc(lb1, 1)
            act.wait_ge(floored, 1)
            act.activation(f_all, f_all, ACT.Ln).then_inc(logged, 1)
            for u in range(N):
                m, j = divmod(u, 2)
                b, k = tile(g.fB[:, j, :], m), u % 2
                act.wait_ge(scanned, 2)
                read_beside()
                act.wait_ge(gap_min, u + 1)
                act.activation(gapsb[k], gapsb[k], ACT.Exp).then_inc(gap_exp, 1)
                act.wait_ge(qg_min, u + 1)
                act.activation(qgap, qgap, ACT.Exp).then_inc(qg_exp, 1)
                if u:
                    act.wait_ge(st_done, 2 * u)
                act.activation(expb, b, ACT.Exp).then_inc(expb_done, 1)
                if u:
                    act.wait_ge(kT_ready, u)
                act.activation(kdec, b, ACT.Exp, bias=b[:, P - 1:P], scale=-1.0).then_inc(klast, 1)
                act.wait_ge(att_ready, u + 1)
                if u >= 2:
                    act.wait_ge(o_ready, u - 1)
                act.activation(att[k], bank[:, k, 0:256].rearrange("p (h n) -> p h n", h=2),
                               ACT.Copy).then_inc(att_read, 1)
                act.wait_ge(kT_ready, u + 1)
                if u:
                    act.wait_ge(u_ready, u)
                act.activation(kdecT, bank[:, 2, 0:P], ACT.Copy).then_inc(kT_read, 1)
                if j:
                    act.wait_ge(o_ready, u + 1)
                    act.activation(o_all[:, m, :], bank[:, 3 + m % 2, 0:256], ACT.Copy).then_inc(o_read, 1)
            read_beside()
            act.wait_ge(kdec_done, N)
            act.activation(gt_buf, g_in, ACT.Tanh, scale=0.5).then_inc(gt, 1)
            act.wait_ge(sse, 1)
            act.activation(ss[:], ss[:], ACT.Sqrt).then_inc(ssq, 1)
            read_beside()
            for m in range(NT):
                act.wait_ge(yT_ready, m + 1)
                for j in range(2):
                    ins = act.activation(tile(g.yT[:, 4 + j, :], m), bank[:, m % 2, j * P:(j + 1) * P], ACT.Copy,
                                         scale=g.normB[:, j:j + 1])
                ins.then_inc(yT_read, 1)
            read_beside(len(beside))

        @block.vector
        def _(dve):
            dve.tensor_tensor(lb[:], g.lbB[:], g.lbB[:], ALU.subtract).then_inc(lb0, 1)
            dve.wait_ge(lb1, 1)
            dve.reciprocal(oml[:], lb[:]).then_inc(lb2, 1)
            dve.wait_ge(lb2, 1)
            dve.tensor_tensor(lb[:], lb[:], oml[:], ALU.mult).then_inc(lb2, 1)
            dve.wait_ge(lb2, 2)
            dve.tensor_tensor(lb[:], lb[:], lb[:], ALU.subtract).then_inc(lb2, 1)
            dve.wait_ge(lb2, 3)
            dve.tensor_scalar(oml[:], lb[:], -1.0, 1.0, ALU.mult, ALU.add).then_inc(lb3, 1)
            dve.wait_ge(lb3, 1)
            dve.wait_ge(sig, 1)
            for j in range(2):
                dve.tensor_scalar(g.fB[:, j, :], g.fB[:, j, :], oml[:, j:j + 1], lb[:, j:j + 1],
                                  ALU.mult, ALU.add).then_inc(gate, 1)
            dve.wait_ge(gate, 2)
            dve.tensor_scalar(key_all, f_all, -1.0, 1.0, ALU.mult, ALU.add).then_inc(keyed, 1)
            dve.wait_ge(keyed, 1)
            dve.tensor_scalar(f_all, f_all, 1e-19, None, ALU.max).then_inc(floored, 1)
            dve.wait_ge(logged, 1)
            dve.wait_ge(cleared, 5)
            for j in range(2):
                dve.tensor_tensor_scan(g.fB[:, j, :], ones_rows, g.fB[:, j, :], 0.0,
                                       ALU.mult, ALU.add).then_inc(scanned, 1)
            dve.wait_ge(scanned, 2)
            for u in range(N):
                m, j = divmod(u, 2)
                k = u % 2
                b, q, kk = tile(g.fB[:, j, :], m), tile(g.qB[:, j, :], m), tile(key[:, j, :], m)
                if u:
                    dve.wait_ge(qz_done, 2 * u)
                dve.tensor_tensor(qgap, b.rearrange("p (i s) -> p i s", i=NSUB),
                                  bcast(mids(j, m).unsqueeze(2), [P, NSUB, SUB]), ALU.subtract).then_inc(qg, 1)
                dve.wait_ge(gap, u + 1)
                dve.tensor_scalar(gapsb[k], gapsb[k], CLAMP, None, ALU.min).then_inc(gap_min, 1)
                dve.wait_ge(qg, u + 1)
                dve.tensor_scalar(qgap, qgap, CLAMP, None, ALU.min).then_inc(qg_min, 1)
                dve.wait_ge(gap_exp, u + 1)
                dve.tensor_tensor(gapsb[k], gapsb[k], bcast(kk.unsqueeze(1), [P, NSUB, P]), ALU.mult).then_inc(kf, 1)
                dve.wait_ge(qg_exp, u + 1)
                if u >= 2:
                    dve.wait_ge(att_ready, u - 1)
                qf = qgap.rearrange("p i s -> p (i s)")
                dve.tensor_tensor(qz[k][0:HD, 0, :], qf[0:HD], q[0:HD], ALU.mult).then_inc(qz_done, 1)
                dve.tensor_tensor(qz[k][HD:P, 1, :], qf[HD:P], q[HD:P], ALU.mult).then_inc(qz_done, 1)
                dve.wait_ge(expb_done, u + 1)
                if u:
                    dve.wait_ge(o_ready, u)
                dve.tensor_tensor(qdec, expb, q, ALU.mult).then_inc(qdec_done, 1)
                dve.wait_ge(klast, u + 1)
                dve.tensor_tensor(kdec, kdec, kk, ALU.mult).then_inc(kdec_done, 1)
                dve.wait_ge(u_ready, u + 1)
                dve.wait_ge(o_ready, u + 1)
                dve.wait_ge(qdec_done, u + 1)
                for h in range(2):
                    r = slice(h * HD, (h + 1) * HD)
                    dve.scalar_tensor_tensor(out=state[r, j, h, :], in0=state[r, j, h, :], scalar=expb[r, P - 1:P],
                                             in1=bank[r, 5, h * HD:(h + 1) * HD],
                                             op0=ALU.mult, op1=ALU.add).then_inc(st_done, 1)
            dve.wait_ge(o_read, NT)
            dve.wait_ge(kf, N)
            dve.tensor_tensor(sq, o_all, o_all, ALU.mult).then_inc(sqd, 1)
            dve.wait_ge(sqd, 1)
            dve.tensor_reduce(ss[:].rearrange("p m h -> p (m h)"),
                              sq.rearrange("p m (h n) -> p (m h) n", h=4), AX.X, ALU.add).then_inc(ssd, 1)
            dve.wait_ge(ssd, 1)
            dve.tensor_scalar(ss[:], ss[:], 1.0 / HD, RMS_EPS, ALU.mult, ALU.add).then_inc(sse, 1)
            dve.wait_ge(gt, 1)
            dve.scalar_tensor_tensor(out=gt_buf, in0=gt_buf, scalar=1.0, in1=g_in,
                                     op0=ALU.add, op1=ALU.mult).then_inc(silu1, 1)
            dve.wait_ge(silu1, 1)
            dve.scalar_tensor_tensor(out=o_all, in0=o_all, scalar=0.5, in1=gt_buf,
                                     op0=ALU.mult, op1=ALU.mult).then_inc(silu2, 1)
            dve.wait_ge(ssq, 1)
            dve.reciprocal(ss[:], ss[:]).then_inc(ssr, 1)
            dve.wait_ge(ssr, 1)
            dve.wait_ge(silu2, 1)
            for m in range(NT):
                o = o_all[:, m, :].rearrange("p (h n) -> p h n", h=4)
                dve.tensor_tensor(o, o, bcast(ss[:, m, :].unsqueeze(2), [P, 4, HD]), ALU.mult).then_inc(n1, 1)

        @block.tensor
        def _(pe):
            fill = filler(g, pe, g.slots_b, g.slots_c)
            fill(8)
            pe.wait_ge(cleared, 5)

            def scores(u):
                if u >= 2:
                    pe.wait_ge(att_read, u - 1)
                pe.wait_ge(kf, u + 1)
                pe.wait_ge(qz_done, 2 * u + 2)
                out = bank[:, u % 2, 0:256].rearrange("p (h n) -> p h n", h=2)
                for i in range(NSUB):
                    s = slice(i * SUB, (i + 1) * SUB)
                    mm = pe.matmul(out[0:s.stop, :, s], gapsb[u % 2][:, i, 0:s.stop], qz[u % 2][:, :, s],
                                   start=True, stop=True)
                mm.then_inc(att_ready, 1)

            def turn_key(u):
                pe.wait_ge(kdec_done, u + 1)
                if u:
                    pe.wait_ge(kT_read, u)
                pe.transpose(bank[:, 2, 0:P], kdec, g.ident[:]).then_inc(kT_ready, 1)

            def outputs(u):
                m, j = divmod(u, 2)
                if j == 0 and m >= 2:
                    pe.wait_ge(o_read, m - 1)
                pe.wait_ge(qdec_done, u + 1)
                if u:
                    pe.wait_ge(st_done, 2 * u)
                out = bank[:, 3 + m % 2, j * P:(j + 1) * P]
                pe.matmul(out, qdec, state[:, j].rearrange("p h n -> p (h n)"), start=True, stop=True,
                          skip_group_check=True)
                pe.wait_ge(att_cut, u + 1)
                for h in range(2):
                    c = (2 * j + h) * HD
                    mm = pe.matmul(out[:, h * HD:(h + 1) * HD], att[u % 2][:, h, :], g.igB[:, m, c:c + HD],
                                   start=False, stop=True, skip_group_check=True)
                mm.then_inc(o_ready, 1)

            def state_sum(u):
                m, j = divmod(u, 2)
                pe.wait_ge(kT_read, u + 1)
                if u:
                    pe.wait_ge(st_done, 2 * u)
                pe.matmul(bank[:, 5, 0:P], kdecT, g.igB[:, m, j * P:(j + 1) * P],
                          start=True, stop=True).then_inc(u_ready, 1)

            for u in range(N):
                fill(4)
                scores(u)
                turn_key(u)
                fill(1)
                state_sum(u)
                fill(3)
                outputs(u)
            fill(8)
            for m in range(NT):
                pe.wait_ge(n1, m + 1)
                if m >= 2:
                    pe.wait_ge(yT_read, m - 1)
                for j in range(2):
                    mm = pe.transpose(bank[:, m % 2, j * P:(j + 1) * P], o_all[:, m, j * P:(j + 1) * P], g.ident[:])
                mm.then_inc(yT_ready, 1)
            fill()



def mix_c(g):
    nc, sem, bank = g.nc, g.sem, g.bank
    xc = g.region(R2, 4, T)
    th = g.region(R2 + 4096, 4, T)
    cz = g.region(R2 + 4096, 2, T)
    o_all = g.region(YT0 + 8192, NT, 256)
    at = WK
    sp_rows, dec_rows, ab = g.region(at, T)[0:8], g.rows[:], g.region(at + 1024, T)[0:8]
    keep = g.region(at + 2048, T)[0:8]
    cols = g.region(at + 1024, NT, 2, 8)
    tm = g.region(at + 1152, 384)
    xdt, xdec = g.region(at + 1536, 256), g.region(at + 1792, 256)
    E = g.region(at + 2048, 4, P)
    att = g.region(at + 2560, 4, P)
    eb = g.region(at + 3072, 2, P)
    cdec = g.region(at + 3328, 2, P)
    state = g.region(at + 3584, 4, HD)
    skip = g.region(at + 3840, 256)
    sel, sel2 = g.region(at + 4096, 4, P)[0:8], g.region(at + 4608, 2, P)[0:8]
    neglog = g.sb("neglog", [8, 1])
    neg_row = g.sb("neg_row", [8, 1])[:]
    ss = g.sb("ssC", [P, NT, 2])
    g.sel_rows = sel
    names = ("halved z0 z1 z2 z3 z4 nl rowsd keepd summed sel colsT colsr conv tanh silu cpad clear tmT tmr xdt "
             "rowsb eb0 CB E eb att cdec xdec y u st skip yr gt s1 s2 sq ss sse ssq ssr n1 yT yTr").split()
    s = {n: sem("c_" + n) for n in names}
    z_all = g.region(R3 + 4 * (T + 3), 2048)
    gt_buf = g.region(R3, NT, 256)

    def tile(ap, m):
        return ap[:, m * P:(m + 1) * P]

    staging = g.region(WK + 4864, HALF)

    with nc.Block() as block:
        @block.sync
        def _(sp):
            spill_gates(g, sp, g.slots_c, g.slots_d, staging)

        @block.gpsimd
        def _(pool):
            pool.memset(keep, 1.0).then_inc(s["keepd"], 1)
            pool.wait_ge(s["keepd"], 1)
            pool.memset(keep[0:4, 0:T:P], 0.0).then_inc(s["keepd"], 1)
            pool.memset(state, 0.0).then_inc(s["clear"], 1)
            pool.wait_ge(s["silu"], 3)
            pool.wait_ge(s["clear"], 1)
            pool.memset(cz, 0.0).then_inc(s["clear"], 1)
            for m in range(NT):
                pool.wait_ge(s["tmr"], m + 1)
                if m:
                    pool.wait_ge(s["yr"], m)
                pool.tensor_tensor(skip.rearrange("p (h n) -> p h n", h=4),
                                   tm[:, 0:256].rearrange("p (h n) -> p h n", h=4),
                                   bcast(g.dskip[:].unsqueeze(2), [P, 4, HD]), ALU.mult).then_inc(s["skip"], 1)

        @block.scalar
        def _(act):
            stage = stager(g, act, g.slots_c, g.slots_d, staging)
            act.activation(neglog[:], g.rowlog[:], ACT.Exp).then_inc(s["nl"], 1)
            act.wait_ge(s["z1"], 1)
            act.activation(ab, g.rows[:], ACT.Abs).then_inc(s["z2"], 1)
            act.wait_ge(s["z2"], 1)
            act.activation(ab, ab, ACT.Exp, scale=-1.0).then_inc(s["z2"], 1)
            act.wait_ge(s["z2"], 2)
            act.activation(ab, ab, ACT.Ln, bias=1.0).then_inc(s["z2"], 1)
            for i in range(4):
                act.wait_ge(s["conv"], 4 * (i + 1))
                act.activation(th[:, i, :], xc[:, i, :], ACT.Tanh).then_inc(s["tanh"], 1)
                stage((i + 1) // 2)
            act.wait_ge(s["colsT"], 1)
            act.activation(cols[:, :, 0, :], bank[:, 5, 0:128].rearrange("p (m a r) -> p m a r", m=NT, a=2)[:, :, 0, :],
                           ACT.Copy).then_inc(s["colsr"], 1)
            act.activation(cols[:, :, 1, :], bank[:, 5, 0:128].rearrange("p (m a r) -> p m a r", m=NT, a=2)[:, :, 1, :],
                           ACT.Copy, scale=-1.0).then_inc(s["colsr"], 1)
            act.wait_ge(s["colsr"], 2)
            for m in range(NT):
                act.wait_ge(s["tmT"], m + 1)
                if m:
                    act.wait_ge(s["u"], m)
                    act.wait_ge(s["skip"], m)
                    act.wait_ge(s["xdt"], m)
                act.activation(tm, bank[:, 0, 0:384], ACT.Copy).then_inc(s["tmr"], 1)
                act.wait_ge(s["rowsb"], m + 1)
                if m:
                    act.wait_ge(s["att"], m)
                    act.wait_ge(s["xdec"], m)
                for h in range(4):
                    act.activation(E[:, h, :], bank[:, 1, h * P:(h + 1) * P], ACT.Exp,
                                   bias=cols[:, m, 1, h:h + 1]).then_inc(s["E"], 1)
                act.wait_ge(s["eb0"], m + 1)
                if m:
                    act.wait_ge(s["cdec"], m)
                    act.wait_ge(s["st"], 4 * m)
                act.activation(eb, bank[:, 2, 0:256].rearrange("p (r n) -> p r n", r=2), ACT.Exp).then_inc(s["eb"], 1)
                stage(m + 2)
            stage(NT + 2)
            act.activation(gt_buf, g.zC, ACT.Tanh, scale=0.5).then_inc(s["gt"], 1)
            act.wait_ge(s["sse"], 1)
            act.activation(ss[:], ss[:], ACT.Sqrt).then_inc(s["ssq"], 1)
            for m in range(NT):
                act.wait_ge(s["yT"], m + 1)
                for j in range(2):
                    ins = act.activation(tile(g.yT[:, 6 + j, :], m), bank[:, m % 2, j * P:(j + 1) * P], ACT.Copy,
                                         scale=g.normC[:, j:j + 1])
                ins.then_inc(s["yTr"], 1)
            stage()

        @block.vector
        def _(dve):
            dve.memset(neg_row, -1.0).then_inc(s["z0"], 1)
            dve.wait_ge(s["z0"], 1)
            dve.memset(neg_row[0:4], 1.0).then_inc(s["z0"], 1)
            dve.wait_ge(s["z0"], 2)
            dve.tensor_scalar(g.rows[:], g.rows[:], g.rowbias[:], neg_row, ALU.add, ALU.mult).then_inc(s["z1"], 1)
            dve.wait_ge(s["z1"], 1)
            dve.wait_ge(s["z2"], 3)
            dve.scalar_tensor_tensor(out=sp_rows, in0=g.rows[:], scalar=0.0, in1=ab,
                                     op0=ALU.max, op1=ALU.add).then_inc(s["z3"], 1)
            dve.wait_ge(s["nl"], 1)
            dve.tensor_scalar(neglog[:], neglog[:], -1.0, None, ALU.mult).then_inc(s["z4"], 1)
            dve.wait_ge(s["z3"], 1)
            dve.wait_ge(s["z4"], 1)
            dve.tensor_scalar(dec_rows, sp_rows, neglog[:], None, ALU.mult).then_inc(s["rowsd"], 1)
            dve.wait_ge(s["rowsd"], 1)
            dve.wait_ge(s["keepd"], 2)
            dve.tensor_tensor_scan(dec_rows, keep, dec_rows, 0.0, ALU.mult, ALU.add).then_inc(s["summed"], 1)
            dve.tensor_copy(sel, bcast(g.ident[0:8, 0:4].unsqueeze(2), [8, 4, P])).then_inc(s["sel"], 1)
            dve.tensor_copy(sel2[:, :, 0:HD], bcast(g.ident[0:8, 0:2].unsqueeze(2), [8, 2, HD])).then_inc(s["sel"], 1)
            dve.tensor_copy(sel2[:, :, HD:P], bcast(g.ident[0:8, 2:4].unsqueeze(2), [8, 2, HD])).then_inc(s["sel"], 1)
            dve.tensor_scalar(g.convw[:], g.convw[:], 0.5, None, ALU.mult).then_inc(s["halved"], 1)
            dve.tensor_scalar(g.convb[:], g.convb[:], 0.5, None, ALU.mult).then_inc(s["halved"], 1)
            dve.wait_ge(s["halved"], 2)
            for i in range(4):
                dve.tensor_scalar(xc[:, i, :], g.cX[:, i, 0:T], g.convw[:, i, 0:1], g.convb[:, i:i + 1],
                                  ALU.mult, ALU.add).then_inc(s["conv"], 1)
                for t in range(1, 4):
                    dve.wait_ge(s["conv"], 4 * i + t)
                    dve.scalar_tensor_tensor(out=xc[:, i, :], in0=g.cX[:, i, t:t + T], scalar=g.convw[:, i, t:t + 1],
                                             in1=xc[:, i, :], op0=ALU.mult, op1=ALU.add).then_inc(s["conv"], 1)
            for i in range(4):
                dve.wait_ge(s["tanh"], i + 1)
                dve.scalar_tensor_tensor(out=xc[:, i, :], in0=th[:, i, :], scalar=1.0, in1=xc[:, i, :],
                                         op0=ALU.add, op1=ALU.mult).then_inc(s["silu"], 1)
            dve.wait_ge(s["silu"], 4)
            dve.wait_ge(s["clear"], 2)
            for h in range(2):
                r = slice(h * HD, (h + 1) * HD)
                dve.tensor_copy(cz[r, h, :], xc[r, 3, :]).then_inc(s["cpad"], 1)
            for m in range(NT):
                dve.wait_ge(s["tmr"], m + 1)
                dve.wait_ge(s["colsr"], 2)
                if m:
                    dve.wait_ge(s["y"], m)
                dve.tensor_tensor(xdt.rearrange("p (h n) -> p h n", h=4),
                                  tm[:, 0:256].rearrange("p (h n) -> p h n", h=4),
                                  bcast(cols[:, m, 0, 0:4].unsqueeze(2), [P, 4, HD]), ALU.mult).then_inc(s["xdt"], 1)
                dve.wait_ge(s["E"], 4 * (m + 1))
                dve.wait_ge(s["CB"], m + 1)
                dve.tensor_tensor(att.rearrange("p (a r) n -> p a r n", a=2),
                                  E.rearrange("p (a r) n -> p a r n", a=2),
                                  bcast(bank[:, 3, 0:256].rearrange("p (a n) -> p a n", a=2).unsqueeze(2),
                                        [P, 2, 2, P]), ALU.mult).then_inc(s["att"], 1)
                dve.wait_ge(s["eb"], m + 1)
                dve.tensor_tensor(cdec, eb, bcast(tile(xc[:, 3, :], m).unsqueeze(1), [P, 2, P]),
                                  ALU.mult).then_inc(s["cdec"], 1)
                dve.wait_ge(s["xdt"], m + 1)
                if m:
                    dve.wait_ge(s["u"], m)
                dve.tensor_tensor(xdec.rearrange("p (h n) -> p h n", h=4), xdt.rearrange("p (h n) -> p h n", h=4),
                                  bcast(E[:, :, P - 1:P], [P, 4, HD]), ALU.mult).then_inc(s["xdec"], 1)
                dve.wait_ge(s["u"], m + 1)
                dve.wait_ge(s["y"], m + 1)
                for h in range(4):
                    a, r = divmod(h, 2)
                    q = slice(a * HD, (a + 1) * HD)
                    dve.scalar_tensor_tensor(out=state[q, h, :], in0=state[q, h, :], scalar=eb[q, r, P - 1:P],
                                             in1=bank[q, 5, h * HD:(h + 1) * HD],
                                             op0=ALU.mult, op1=ALU.add).then_inc(s["st"], 1)
                dve.wait_ge(s["skip"], m + 1)
                dve.tensor_tensor(o_all[:, m, :], bank[:, 4, 0:256], skip, ALU.add).then_inc(s["yr"], 1)
            dve.wait_ge(s["gt"], 1)
            dve.scalar_tensor_tensor(out=gt_buf, in0=gt_buf, scalar=1.0, in1=g.zC,
                                     op0=ALU.add, op1=ALU.mult).then_inc(s["s1"], 1)
            dve.wait_ge(s["s1"], 1)
            dve.wait_ge(s["yr"], NT)
            dve.scalar_tensor_tensor(out=o_all, in0=o_all, scalar=0.5, in1=gt_buf,
                                     op0=ALU.mult, op1=ALU.mult).then_inc(s["s2"], 1)
            dve.wait_ge(s["s2"], 1)
            dve.tensor_tensor(gt_buf, o_all, o_all, ALU.mult).then_inc(s["sq"], 1)
            dve.wait_ge(s["sq"], 1)
            dve.tensor_reduce(ss[:].rearrange("p m h -> p (m h)"),
                              gt_buf.rearrange("p m (h n) -> p (m h) n", h=2), AX.X, ALU.add).then_inc(s["ss"], 1)
            dve.wait_ge(s["ss"], 1)
            dve.tensor_scalar(ss[:], ss[:], 1.0 / P, RMS_EPS, ALU.mult, ALU.add).then_inc(s["sse"], 1)
            dve.wait_ge(s["ssq"], 1)
            dve.reciprocal(ss[:], ss[:]).then_inc(s["ssr"], 1)
            dve.wait_ge(s["ssr"], 1)
            for m in range(NT):
                o = o_all[:, m, :].rearrange("p (h n) -> p h n", h=2)
                dve.tensor_tensor(o, o, bcast(ss[:, m, :].unsqueeze(2), [P, 2, P]), ALU.mult).then_inc(s["n1"], 1)

        @block.tensor
        def _(pe):
            fill = filler(g, pe, g.slots_c, g.slots_d)
            fill(20)
            pe.wait_ge(s["summed"], 1)
            for m in range(NT):
                pe.transpose(bank[:, 5, 16 * m:16 * m + 8], tile(sp_rows, m), g.ident[0:8, 0:8])
                mm = pe.transpose(bank[:, 5, 16 * m + 8:16 * m + 16], tile(dec_rows, m), g.ident[0:8, 0:8])
            mm.then_inc(s["colsT"], 1)
            pe.wait_ge(s["sel"], 3)
            pe.wait_ge(s["colsr"], 2)
            pe.wait_ge(s["silu"], 4)
            pe.wait_ge(s["cpad"], 2)
            for m in range(NT):
                if m:
                    pe.wait_ge(s["tmr"], m)
                for i in range(3):
                    mm = pe.transpose(bank[:, 0, i * P:(i + 1) * P], tile(xc[:, i, :], m), g.ident[:])
                mm.then_inc(s["tmT"], 1)
                if m:
                    pe.wait_ge(s["E"], 4 * m)
                pe.matmul(bank[:, 1, :], g.ident[:], bcast(g.neg_below[:].unsqueeze(1), [P, 4, P]),
                          start=True, stop=True, skip_group_check=True)
                for h in range(4):
                    mm = pe.matmul(bank[:, 1, h * P:(h + 1) * P], sel[:, h, :], tile(dec_rows, m),
                                   start=False, stop=True, skip_group_check=True)
                mm.then_inc(s["rowsb"], 1)
                if m:
                    pe.wait_ge(s["eb"], m)
                for r in range(2):
                    mm = pe.matmul(bank[:, 2, r * P:(r + 1) * P], sel2[:, r, :], tile(dec_rows, m),
                                   start=True, stop=True)
                mm.then_inc(s["eb0"], 1)
                fill(2)
                if m:
                    pe.wait_ge(s["att"], m)
                pe.matmul(bank[:, 3, 0:256], tile(xc[:, 2, :], m), cz[:, :, m * P:(m + 1) * P],
                          start=True, stop=True).then_inc(s["CB"], 1)
                fill(3)
                pe.wait_ge(s["cdec"], m + 1)
                if m:
                    pe.wait_ge(s["st"], 4 * m)
                    pe.wait_ge(s["yr"], m)
                else:
                    pe.wait_ge(s["clear"], 1)
                y = bank[:, 4, 0:256].rearrange("p (h n) -> p h n", h=4)
                for r in range(2):
                    pe.matmul(y[:, r::2, :], cdec[:, r, :], state[:, r::2, :],
                              start=(r == 0), stop=True, skip_group_check=True)
                pe.wait_ge(s["att"], m + 1)
                pe.wait_ge(s["xdt"], m + 1)
                for h in range(4):
                    mm = pe.matmul(y[:, h, :], att[:, h, :], xdt[:, h * HD:(h + 1) * HD],
                                   start=False, stop=True, skip_group_check=True)
                mm.then_inc(s["y"], 1)
                fill(3)
                pe.wait_ge(s["xdec"], m + 1)
                pe.matmul(bank[:, 5, 0:256], tm[:, 256:384], xdec, start=True, stop=True).then_inc(s["u"], 1)
            fill(16)
            for m in range(NT):
                pe.wait_ge(s["n1"], m + 1)
                if m >= 2:
                    pe.wait_ge(s["yTr"], m - 1)
                for j in range(2):
                    mm = pe.transpose(bank[:, m % 2, j * P:(j + 1) * P], o_all[:, m, j * P:(j + 1) * P], g.ident[:])
                mm.then_inc(s["yT"], 1)
            fill()



def mix_d(g):
    nc, sem, bank = g.nc, g.sem, g.bank
    N = 4 * NT
    probs = [g.region(WK + 1024 * i, T) for i in range(2)]
    probsT = [g.region(WK + 2048 + 1024 * i, NT, P) for i in range(2)]
    y = g.region(WK + 4096, 256)
    sel = g.region(WK + 4352, 4, P)[0:8]
    mx, neg = g.sb("maxD", [P, NT, 4]), g.sb("negD", [P, NT, 4])
    den = g.sb("denD", [P, NT, 4])
    s = {n: sem("d_" + n) for n in
                           "sel S mx neg P pT pTr pv rd y yT yTr".split()}

    def groups(i):
        return [range(a, min(a + 4, i + 1)) for a in range(0, i + 1, 4)]

    first_turn = [sum(len(groups(v // 4)) for v in range(u)) for u in range(N + 1)]

    staging = g.region(WK + 4864, HALF)

    with nc.Block() as block:
        @block.sync
        def _(sp):
            spill_gates(g, sp, g.slots_d, g.slots_merge, staging)

        @block.tensor
        def _(pe):
            fill = filler(g, pe, g.slots_d, g.slots_merge)
            pe.wait_ge(s["sel"], 1)

            def score(u):
                i, h = divmod(u, 4)
                if u >= 2:
                    pe.wait_ge(s["P"], u - 1)
                    pe.wait_ge(s["mx"], u - 1)
                for c in range(0, (i + 1) * P, HALF):
                    n = min(HALF, (i + 1) * P - c)
                    out = bank[:, 2 * (u % 2) + c // HALF, 0:n]
                    pe.matmul(out, g.qD[:, h // 2, i * P:(i + 1) * P], g.kD[:, h // 2, h % 2, c:c + n],
                              start=True, stop=True, skip_group_check=True)
                    mm = pe.matmul(out, sel[:, h, :], g.rows[:, c:c + n],
                                   start=False, stop=True, skip_group_check=True)
                out = bank[:, 2 * (u % 2) + i // 4, (i % 4) * P:(i % 4 + 1) * P]
                pe.matmul(out, g.ident[:], g.neg_above[:], start=False, stop=True,
                          skip_group_check=True).then_inc(s["S"], 1)

            def turn(u):
                i, h = divmod(u, 4)
                pe.wait_ge(s["P"], u + 1)
                for c, tiles in enumerate(groups(i)):
                    n = first_turn[u] + c
                    if n:
                        pe.wait_ge(s["pTr"], n)
                    for kt in tiles:
                        mm = pe.transpose(bank[:, 4, (kt % 4) * P:(kt % 4 + 1) * P],
                                          probs[u % 2][:, kt * P:(kt + 1) * P], g.ident[:])
                    mm.then_inc(s["pT"], 1)

            def values(u):
                i, h = divmod(u, 4)
                pe.wait_ge(s["pTr"], first_turn[u + 1])
                if h == 0 and i:
                    pe.wait_ge(s["yTr"], i)
                for kt in range(i + 1):
                    mm = pe.matmul(bank[:, 5, h * HD:(h + 1) * HD], probsT[u % 2][:, kt, :],
                                   g.vD[:, kt, h * HD:(h + 1) * HD], start=(kt == 0), stop=(kt == i))
                mm.then_inc(s["pv"], 1)

            def turn_y(i):
                pe.wait_ge(s["y"], i + 1)
                for c in range(2):
                    mm = pe.transpose(bank[:, 5, c * P:(c + 1) * P], y[:, c * P:(c + 1) * P], g.ident[:])
                mm.then_inc(s["yT"], 1)

            for i in range(N + 2):
                if i < N:
                    score(i)
                fill(2)
                if 1 <= i < N + 1:
                    turn(i - 1)
                fill(3)
                if i >= 2:
                    values(i - 2)
                    if (i - 2) % 4 == 3:
                        turn_y((i - 2) // 4)
            fill()

        @block.vector
        def _(dve):
            dve.tensor_scalar(sel, bcast(g.ident[0:8, 4:8].unsqueeze(2), [8, 4, P]), -8.0, None,
                              ALU.mult).then_inc(s["sel"], 1)

            def maxes(u):
                i, h = divmod(u, 4)
                dve.wait_ge(s["S"], u + 1)
                flat = bank[:, 2 * (u % 2):2 * (u % 2) + 2, :].rearrange("p b n -> p (b n)")
                dve.tensor_reduce(mx[:, i, h:h + 1], flat[:, 0:(i + 1) * P], AX.X, ALU.max).then_inc(s["mx"], 1)
                dve.wait_ge(s["mx"], u + 1)
                dve.tensor_scalar(neg[:, i, h:h + 1], mx[:, i, h:h + 1], -0.125, None, ALU.mult).then_inc(s["neg"], 1)

            def turned(u):
                i, h = divmod(u, 4)
                if u >= 2:
                    dve.wait_ge(s["pv"], u - 1)
                for c, tiles in enumerate(groups(i)):
                    dve.wait_ge(s["pT"], first_turn[u] + c + 1)
                    dve.tensor_copy(probsT[u % 2][:, tiles.start:tiles.stop, :].rearrange("p a n -> p (a n)"),
                                    bank[:, 4, 0:len(tiles) * P]).then_inc(s["pTr"], 1)

            def norm(i):
                dve.wait_ge(s["P"], 4 * i + 4)
                dve.reciprocal(den[:, i], den[:, i]).then_inc(s["rd"], 1)
                dve.wait_ge(s["rd"], i + 1)
                dve.wait_ge(s["pv"], 4 * i + 4)
                if i:
                    dve.wait_ge(s["yT"], i)
                dve.tensor_tensor(y.rearrange("p (h n) -> p h n", h=4),
                                  bank[:, 5, 0:256].rearrange("p (h n) -> p h n", h=4),
                                  bcast(den[:, i].unsqueeze(2), [P, 4, HD]), ALU.mult).then_inc(s["y"], 1)

            for i in range(N + 2):
                if i < N:
                    maxes(i)
                if 1 <= i < N + 1:
                    turned(i - 1)
                if i >= 2 and (i - 2) % 4 == 3:
                    norm((i - 2) // 4)

        @block.scalar
        def _(act):
            def read_yT(i):
                act.wait_ge(s["yT"], i + 1)
                act.activation(g.yT[:, 8:10, i * P:(i + 1) * P],
                               bank[:, 5, 0:256].rearrange("p (c n) -> p c n", c=2), ACT.Copy).then_inc(s["yTr"], 1)

            stage = stager(g, act, g.slots_d, g.slots_merge, staging)
            for u in range(N):
                i, h = divmod(u, 4)
                act.wait_ge(s["neg"], u + 1)
                if u >= 2:
                    act.wait_ge(s["pT"], first_turn[u - 1])
                flat = bank[:, 2 * (u % 2):2 * (u % 2) + 2, :].rearrange("p b n -> p (b n)")
                act.activation(probs[u % 2][:, 0:(i + 1) * P], flat[:, 0:(i + 1) * P], ACT.Exp, scale=0.125,
                               bias=neg[:, i, h:h + 1], accum_out=den[:, i, h:h + 1]).then_inc(s["P"], 1)
                stage(5 * u // KT)
                if u >= 5 and (u - 5) % 4 == 0:
                    read_yT((u - 5) // 4)
            read_yT(NT - 1)
            stage()



WBR = R1
MERGED = WBR + 10 * D
WOUT = MERGED + KT * T


def merge(g):
    nc, sem, bank = g.nc, g.sem, g.bank
    banks = (6, 7)
    N, S = len(g.gate_unit), 4 * SPILLED
    order = sorted(range(N), key=lambda v: (v + 0.5) / S if v < S else (v - S) / (N - S))
    assert SPILLED % 4 == 0
    wbr, merged = g.region(WBR, 10, D), g.region(MERGED, KT, T)
    sig = [g.region(WOUT + KT * D + HALF * i, HALF) for i in range(3)]
    tiles = [range(0, 4), range(4, 6), range(6, 8), range(8, 10)]
    s = {n: sem("m_" + n) for n in "wbr br sig prod sum".split()}
    gate_in = [sem(f"gate_in{i}") for i in range(3)]
    back = [0, 0, 0]
    wout_in = g.keep("wout_in")
    g.wout_in = wout_in

    def place(v):
        q, i = divmod(v, 4)
        jj, b = divmod(q, 4)
        return 2 * jj + i // 2, b, i % 2

    with nc.Block() as block:
        @block.sync
        def _(sp):
            for a, w in zip(tiles, (g.ins["w_br_a"], g.ins["w_br_b"], g.ins["w_br_c"], g.ins["w_br_d"])):
                sp.dma_start(wbr[:, a.start:a.stop, :], w[0].rearrange("(k p) n -> p k n", p=P)).then_inc(s["wbr"], 16)
            for p, v in enumerate(order):
                if p == 3:
                    sp.dma_start(g.region(WOUT, KT, D),
                                 g.ins["w_out"][0].rearrange("(k p) n -> p k n", p=P)).then_inc(wout_in, 16)
                if v < S:
                    if p >= 3:
                        sp.wait_ge(s["sum"], p - 2)
                    sp.dma_start(sig[p % 3], g.gates[v]).then_inc(gate_in[p % 3], 16)
                elif v % 4 == 3:
                    n = g.U[g.gate_unit[v]][0]
                    if n + 2 < len(g.S):
                        load_slot(g, sp, n + 2)

        @block.tensor
        def _(pe):
            for p, v in enumerate(order):
                j, b, h = place(v)
                if v >= S:
                    project_unit(g, pe, g.gate_unit[v], banks)
                if p == 0:
                    pe.wait_ge(s["wbr"], 64)
                if p >= 2:
                    pe.wait_ge(s["prod"], p - 1)
                for k in tiles[b]:
                    mm = pe.matmul(bank[:, 4 + p % 2, :], wbr[:, k, j * P:(j + 1) * P],
                                   g.yT[:, k, h * HALF:(h + 1) * HALF],
                                   start=(k == tiles[b][0]), stop=(k == tiles[b][-1]))
                mm.then_inc(s["br"], 1)

        @block.scalar
        def _(act):
            for p, v in enumerate(order):
                if v < S:
                    back[p % 3] += 1
                    act.wait_ge(gate_in[p % 3], 16 * back[p % 3])
                    act.activation(sig[p % 3], sig[p % 3], ACT.Sigmoid).then_inc(s["sig"], 1)
                else:
                    u = g.gate_unit[v]
                    act.wait_ge(g.proj_ready, u + 1)
                    if p >= 3:
                        act.wait_ge(s["sum"], p - 2)
                    act.activation(sig[p % 3], proj_bank(g, u, banks), ACT.Sigmoid).then_inc(g.proj_read, 1)

        @block.vector
        def _(dve):
            read = 0
            for p, v in enumerate(order):
                if v < S:
                    read += 1
                    dve.wait_ge(s["sig"], read)
                else:
                    dve.wait_ge(g.proj_read, g.gate_unit[v] + 1)
                dve.wait_ge(s["br"], p + 1)
                dve.tensor_tensor(sig[p % 3], sig[p % 3], bank[:, 4 + p % 2, :], ALU.mult).then_inc(s["prod"], 1)

        @block.gpsimd
        def _(pool):
            for p, v in enumerate(order):
                j, b, h = place(v)
                pool.wait_ge(s["prod"], p + 1)
                dst = merged[:, j, h * HALF:(h + 1) * HALF]
                if b == 0:
                    pool.tensor_copy(dst, sig[p % 3]).then_inc(s["sum"], 1)
                else:
                    pool.wait_ge(s["sum"], p)
                    pool.tensor_tensor(dst, dst, sig[p % 3], ALU.add).then_inc(s["sum"], 1)



BASE = YT0
SHARED = R1
LISTS = 47104


def out_norm(g):
    nc, sem, bank = g.nc, g.sem, g.bank
    merged, wout = g.region(MERGED, KT, T), g.region(WOUT, KT, D)
    wgu, wdn = g.region(SHARED, KT, 512), g.region(SHARED + 4096, 2, D)
    wr = g.region(SHARED + 6144, KT, NE)
    g1, b1 = g.region(SHARED + 6656, D), g.region(SHARED + 7680, D)
    h1 = [g.region(W0 + D * i, D) for i in range(2)]
    h1T = [g.region(W0 + 2 * D + D * i, KT, P) for i in range(2)]
    hid, hidT, silu = g.region(YT0 + 8192, FF), g.region(YT0 + 8448, 2, P), g.region(YT0 + 8704, FF)
    scaled = g.region(YT0 + 8960, P)
    base = g.region(BASE, NT, D)
    g.base, g.logits = base, g.region(SHARED + 8704, NT, NE)
    stats, mv = g.stats, g.mv = g.sb("stats1", [P, 2, 6]), g.sb("mv1", [P, 2])
    rstd = g.rstd = g.sb("rstd1", [P, 1])
    g.h1_rows = nc.dram_tensor("h1_rows", [T, D], F32, kind="Internal").ap()
    g.h1_stored = [g.keep("h1_stored0"), g.keep("h1_stored1")]
    s = {n: sem("o_" + n) for n in (
        "w scaled mix st ag ve sd rs xn g b T0 Tr lg lgr gu si hid hT hTr dn base").split()}
    flat2 = lambda a: bank[:, a:a + 2, :].rearrange("p b n -> p (b n)")

    with nc.Block() as block:
        @block.sync
        def _(sp):
            def row(a):
                return a.rearrange("(a n) -> a n", a=1).to_broadcast([P, D])
            loads = [(wgu[:, :, 0:FF], g.ins["w_sh_gate"][0].rearrange("(k p) n -> p k n", p=P)),
                     (wgu[:, :, FF:], g.ins["w_sh_up"][0].rearrange("(k p) n -> p k n", p=P)),
                     (wdn, g.ins["w_sh_down"][0].rearrange("(k p) n -> p k n", p=P)),
                     (wr, g.ins["w_router"][0].rearrange("(k p) n -> p k n", p=P)),
                     (g1, row(g.ins["ln1_g"][0])), (b1, row(g.ins["ln1_b"][0]))]
            for dst, src in loads:
                sp.dma_start(dst, src).then_inc(s["w"], 16)
            for m in range(NT):
                sp.wait_ge(s["b"], m + 1)
                sp.dma_start(g.h1_rows[m * P:(m + 1) * P, :], h1[m % 2]).then_inc(g.h1_stored[m % 2], 16)

        @block.tensor
        def _(pe):
            pe.wait_ge(g.wout_in, 16)
            pe.wait_ge(s["scaled"], 1)

            def mix(m):
                if m:
                    pe.wait_ge(s["xn"], m)
                for h in range(2):
                    for k in range(KT):
                        pe.matmul(bank[:, h, :], merged[:, k, m * P:(m + 1) * P],
                                  wout[:, k, h * HALF:(h + 1) * HALF],
                                  start=(k == 0), stop=True, skip_group_check=True)
                    for c in range(4):
                        mm = pe.matmul(bank[:, h, c * P:(c + 1) * P], g.hT[:, 4 * h + c, m * P:(m + 1) * P],
                                       scaled, start=False, stop=True, skip_group_check=True)
                mm.then_inc(s["mix"], 1)

            def turn(m):
                pe.wait_ge(s["b"], m + 1)
                if m:
                    pe.wait_ge(s["Tr"], m)
                for k in range(KT):
                    mm = pe.transpose(bank[:, 2 + k // 4, (k % 4) * P:(k % 4 + 1) * P],
                                      h1[m % 2][:, k * P:(k + 1) * P], g.ident[:])
                mm.then_inc(s["T0"], 1)

            def up(m):
                pe.wait_ge(s["Tr"], m + 1)
                if m:
                    pe.wait_ge(s["lgr"], m)
                    pe.wait_ge(s["hid"], m)
                else:
                    pe.wait_ge(s["w"], 96)
                for k in range(KT):
                    mm = pe.matmul(bank[:, 4, 0:NE], h1T[m % 2][:, k, :], wr[:, k, :],
                                   start=(k == 0), stop=(k == KT - 1))
                mm.then_inc(s["lg"], 1)
                for k in range(KT):
                    mm = pe.matmul(bank[:, 5, :], h1T[m % 2][:, k, :], wgu[:, k, :],
                                   start=(k == 0), stop=(k == KT - 1))
                mm.then_inc(s["gu"], 1)

            def down(m):
                pe.wait_ge(s["hid"], m + 1)
                pe.wait_ge(s["lgr"], m + 1)
                for k in range(2):
                    mm = pe.transpose(bank[:, 4, (1 + k) * P:(2 + k) * P], hid[:, k * P:(k + 1) * P], g.ident[:])
                mm.then_inc(s["hT"], 1)
                pe.wait_ge(s["hTr"], m + 1)
                if m:
                    pe.wait_ge(s["base"], m)
                for h in range(2):
                    for k in range(2):
                        mm = pe.matmul(bank[:, 6 + h, :], hidT[:, k, :], wdn[:, k, h * HALF:(h + 1) * HALF],
                                       start=(k == 0), stop=(k == 1))
                mm.then_inc(s["dn"], 1)

            for m in range(NT + 1):
                if m < NT:
                    mix(m)
                if m:
                    turn(m - 1)
                    up(m - 1)
                    down(m - 1)

        @block.vector
        def _(dve):
            dve.tensor_scalar(scaled, g.ident[:], ALPHA, None, ALU.mult).then_inc(s["scaled"], 1)
            dve.wait_ge(s["w"], 96)

            def norm(m):
                dve.wait_ge(s["mix"], m + 1)
                for h in range(2):
                    dve.bn_stats(stats[:, h, :], bank[:, h, :]).then_inc(s["st"], 1)
                dve.wait_ge(s["st"], 2 * (m + 1))
                dve.bn_aggr(mv[:], stats[:]).then_inc(s["ag"], 1)
                dve.wait_ge(s["ag"], m + 1)
                dve.tensor_scalar(rstd[:], mv[:, 1:2], LN_EPS, None, ALU.add).then_inc(s["ve"], 1)
                dve.wait_ge(s["sd"], m + 1)
                dve.reciprocal(rstd[:], rstd[:]).then_inc(s["rs"], 1)
                dve.wait_ge(s["rs"], m + 1)
                if m >= 2:
                    dve.wait_ge(s["T0"], m - 1)
                    dve.wait_ge(s["base"], m - 1)
                    dve.wait_ge(g.h1_stored[m % 2], 16 * (m // 2))
                dve.tensor_scalar(h1[m % 2], flat2(0), mv[:, 0:1], rstd[:], ALU.subtract, ALU.mult).then_inc(s["xn"], 1)

            def rest(m):
                dve.wait_ge(s["gu"], m + 1)
                dve.wait_ge(s["si"], m + 1)
                if m:
                    dve.wait_ge(s["hT"], m)
                dve.tensor_tensor(hid, silu, bank[:, 5, FF:], ALU.mult).then_inc(s["hid"], 1)
                dve.wait_ge(s["dn"], m + 1)
                dve.scalar_tensor_tensor(out=base[:, m, :], in0=h1[m % 2], scalar=ALPHA, in1=flat2(6),
                                         op0=ALU.mult, op1=ALU.add).then_inc(s["base"], 1)

            for m in range(NT + 1):
                if m < NT:
                    norm(m)
                if m:
                    rest(m - 1)

        @block.gpsimd
        def _(pool):
            pool.wait_ge(s["w"], 96)
            for m in range(NT):
                pool.wait_ge(s["xn"], m + 1)
                pool.tensor_tensor(h1[m % 2], h1[m % 2], g1, ALU.mult).then_inc(s["g"], 1)
                pool.wait_ge(s["g"], m + 1)
                pool.tensor_tensor(h1[m % 2], h1[m % 2], b1, ALU.add).then_inc(s["b"], 1)

        @block.scalar
        def _(act):
            def std(m):
                act.wait_ge(s["ve"], m + 1)
                act.activation(rstd[:], rstd[:], ACT.Sqrt).then_inc(s["sd"], 1)

            std(0)
            for m in range(NT):
                act.wait_ge(s["T0"], m + 1)
                if m >= 2:
                    act.wait_ge(s["gu"], m - 1)
                act.activation(h1T[m % 2].rearrange("p k n -> p (k n)"), flat2(2), ACT.Copy).then_inc(s["Tr"], 1)
                if m + 1 < NT:
                    std(m + 1)
                act.wait_ge(s["lg"], m + 1)
                act.activation(g.logits[:, m, :], bank[:, 4, 0:NE], ACT.Copy).then_inc(s["lgr"], 1)
                act.wait_ge(s["gu"], m + 1)
                if m:
                    act.wait_ge(s["hid"], m)
                act.activation(silu, bank[:, 5, 0:FF], ACT.Silu).then_inc(s["si"], 1)
                act.wait_ge(s["hT"], m + 1)
                if m:
                    act.wait_ge(s["dn"], m)
                act.activation(hidT.rearrange("p k n -> p (k n)"), bank[:, 4, P:3 * P], ACT.Copy).then_inc(s["hTr"], 1)



def route(g):
    nc, sem, bank = g.nc, g.sem, g.bank
    at = 0
    def take(*dims):
        nonlocal at
        ap = g.region(at, *dims)
        at += int(np.prod(dims))
        return ap
    scores, sel, pen = take(NT, NE), take(NT, NE), take(NT, GROUPS)
    top2, gsum = take(NT, GROUPS, 8), take(NT, GROUPS)
    gtop, ttop = take(NT, 8), take(NT, 8)
    gidx, tidx = g.sb("gidx", [P, NT, 8], U32), g.sb("tidx", [P, NT, 8], U32)
    gidf, tidf = take(NT, 8), take(NT, 8)
    iota64, iota8 = take(NE), take(GROUPS)
    chosen, prefix, wsel = take(NT, NE), take(NT, NE), take(NT, NE)
    wsum, restart = take(NT), take(NT, NE)
    place, over, extra = take(NT, NE), take(NE), take(NE)
    ovend, ovstart, ovcount = take(NE), take(NE), take(NE)
    before, ones = take(P), take(P)
    tok1, iota48 = take(NT), take(48)
    hot = g.region(R1, NT, TOPK, NE)
    hotg = g.region(R1, NT, TOPG, GROUPS)
    ovhot = g.region(R1 + 3072, 48, NE)
    ovh2 = g.region(R1, 48, NE)
    g.values = g.region(LISTS + 512, NT * NE * 9 // 2).bitcast(BF16).rearrange(
        "p (m e v k) -> p m e v k", m=NT, e=NE, v=3)
    g.pos = g.region(LISTS + 2816, NT, NE)
    exact, dest = take(NT, NE), take(NT, NE)
    rbias = take(NE)
    assert at <= KT * T
    g.shift, g.iota = g.sb("shift", [P, 48]), g.sb("iota", [P, P])
    g.ovexp, g.ovn = g.sb("ovexp", [P, 48], I32), g.sb("ovn", [P, 1], I32)
    ovef = g.region(LISTS, 48)
    s = {n: sem("r_" + n) for n in "rb k0 k1 sc ch cnt fin".split()}
    step = [0]
    g.exp_in = [g.keep(f"exp_in{i}") for i in range(4)]

    with nc.Block() as block:
        @block.sync
        def _(sp):
            sp.dma_start(rbias, g.ins["router_bias"][0].rearrange("(a n) -> a n", a=1).to_broadcast([P, NE])).then_inc(s["rb"], 16)
            for e in range(3):
                load_expert(g, sp, e)
            sp.wait_ge(s["sc"], 1)
            load_expert(g, sp, 3)

        @block.gpsimd
        def _(pool):
            pool.iota(iota64, pattern=[[1, NE]], base=0, channel_multiplier=0,
                      allow_small_or_imprecise_dtypes=True).then_inc(s["k0"], 1)
            pool.iota(iota8, pattern=[[1, GROUPS]], base=0, channel_multiplier=0,
                      allow_small_or_imprecise_dtypes=True).then_inc(s["k0"], 1)
            pool.iota(iota48, pattern=[[1, 48]], base=0, channel_multiplier=0,
                      allow_small_or_imprecise_dtypes=True).then_inc(s["k0"], 1)
            pool.iota(g.iota[:], pattern=[[1, P]], base=0, channel_multiplier=0,
                      allow_small_or_imprecise_dtypes=True).then_inc(s["k0"], 1)
            pool.iota(tok1, pattern=[[P, NT]], base=1, channel_multiplier=1,
                      allow_small_or_imprecise_dtypes=True).then_inc(s["k0"], 1)
            pool.memset(ones, 1.0).then_inc(s["k0"], 1)
            pool.memset(g.values, 0.0).then_inc(s["k0"], 1)
            pool.memset(before, 1.0).then_inc(s["k0"], 1)
            pool.memset(restart, 1.0).then_inc(s["k0"], 1)
            pool.wait_ge(s["k0"], 9)
            pool.affine_select(out=before, in_=before, compare_op=ALU.is_gt, fill=0.0, base=0,
                               pattern=[[1, P]], channel_multiplier=-1).then_inc(s["k1"], 1)
            pool.memset(restart[:, :, 0:1], 0.0).then_inc(s["k1"], 1)

        @block.scalar
        def _(act):
            act.activation(scores, g.logits, ACT.Sigmoid).then_inc(s["sc"], 1)

        @block.tensor
        def _(pe):
            pe.wait_ge(s["k1"], 1)
            pe.wait_ge(s["ch"], 1)
            for m in range(NT):
                mm = pe.matmul(bank[:, 0, m * NE:(m + 1) * NE], before, chosen[:, m, :],
                               start=True, stop=(m == 0))
                for a in range(m):
                    mm = pe.matmul(bank[:, 0, m * NE:(m + 1) * NE], ones, chosen[:, a, :],
                                   start=False, stop=(a == m - 1))
            for m in range(NT):
                mm = pe.matmul(bank[:, 1, 0:NE], ones, chosen[:, m, :], start=(m == 0), stop=(m == NT - 1))
            mm.then_inc(s["cnt"], 1)

        @block.vector
        def _(dve):
            chain = s["fin"]

            def then(ins):
                step[0] += 1
                ins.then_inc(chain, 1)
                dve.wait_ge(chain, step[0])

            dve.wait_ge(s["rb"], 16)
            dve.wait_ge(s["sc"], 1)
            dve.wait_ge(s["k1"], 2)
            then(dve.tensor_tensor(sel, scores, bcast(rbias.unsqueeze(1), [P, NT, NE]), ALU.add))
            for m in range(NT):
                for a in range(GROUPS):
                    ins = dve.max(top2[:, m, a, :], sel[:, m, a * 8:(a + 1) * 8])
            then(ins)
            then(dve.tensor_tensor(gsum, top2[:, :, :, 0], top2[:, :, :, 1], ALU.add))
            for m in range(NT):
                ins = dve.max(gtop[:, m, :], gsum[:, m, :])
            then(ins)
            for m in range(NT):
                ins = dve.max_index(gidx[:, m, :], gtop[:, m, :], gsum[:, m, :])
            then(ins)
            then(dve.tensor_copy(gidf, gidx[:]))
            then(dve.tensor_tensor(hotg, bcast(gidf[:, :, 0:TOPG].unsqueeze(3), [P, NT, TOPG, GROUPS]),
                                   bcast(iota8.unsqueeze(1).unsqueeze(1), [P, NT, TOPG, GROUPS]), ALU.is_equal))
            then(dve.tensor_reduce(pen, hotg.rearrange("p m k e -> p m e k"), AX.X, ALU.add))
            then(dve.tensor_scalar(pen, pen, 1.0, -NEG, ALU.subtract, ALU.mult))
            then(dve.tensor_tensor(sel.rearrange("p m (a e) -> p m a e", a=GROUPS),
                                   sel.rearrange("p m (a e) -> p m a e", a=GROUPS),
                                   bcast(pen.unsqueeze(3), [P, NT, GROUPS, 8]), ALU.add))
            for m in range(NT):
                ins = dve.max(ttop[:, m, :], sel[:, m, :])
            then(ins)
            for m in range(NT):
                ins = dve.max_index(tidx[:, m, :], ttop[:, m, :], sel[:, m, :])
            then(ins)
            then(dve.tensor_copy(tidf, tidx[:]))
            then(dve.tensor_tensor(hot, bcast(tidf[:, :, 0:TOPK].unsqueeze(3), [P, NT, TOPK, NE]),
                                   bcast(iota64.unsqueeze(1).unsqueeze(1), [P, NT, TOPK, NE]), ALU.is_equal))
            dve.tensor_reduce(chosen, hot.rearrange("p m k e -> p m e k"), AX.X, ALU.add).then_inc(s["ch"], 1)
            dve.wait_ge(s["ch"], 1)
            then(dve.tensor_tensor(wsel, scores, chosen, ALU.mult))
            then(dve.tensor_reduce(wsum, wsel, AX.X, ALU.add))
            then(dve.reciprocal(wsum, wsum))
            then(dve.tensor_scalar(wsum, wsum, ROUTED_SCALE, None, ALU.mult))
            then(dve.tensor_tensor(wsel, wsel, bcast(wsum.unsqueeze(2), [P, NT, NE]), ALU.mult))

            def parts(v, x, n):
                for k in range(n):
                    then(dve.tensor_copy(g.values[:, :, :, v, k], x))
                    if k < n - 1:
                        then(dve.tensor_tensor(exact, x, g.values[:, :, :, v, k], ALU.subtract))
                        x = exact

            parts(2, wsel, 3)
            then(dve.tensor_tensor_scan(prefix.rearrange("p m e -> p (m e)"), restart.rearrange("p m e -> p (m e)"),
                                        chosen.rearrange("p m e -> p (m e)"), 0.0, ALU.mult, ALU.add))
            then(dve.tensor_tensor(prefix, prefix, chosen, ALU.subtract))
            tokens = bcast(tok1.unsqueeze(2), [P, NT, NE])
            parts(0, tokens, 2)
            then(dve.scalar_tensor_tensor(out=dest, in0=prefix, scalar=float(T), in1=tokens,
                                          op0=ALU.mult, op1=ALU.add))
            parts(1, dest, 2)
            dve.wait_ge(s["cnt"], 1)
            then(dve.scalar_tensor_tensor(out=place, in0=bank[:, 0, :].rearrange("p (m e) -> p m e", m=NT),
                                          scalar=1.0, in1=chosen, op0=ALU.add, op1=ALU.mult))
            then(dve.tensor_scalar(g.pos, place, -1.0, None, ALU.add))
            then(dve.tensor_scalar(over, bank[:, 1, 0:NE], float(P), None, ALU.is_gt))
            for j in range(2, NT):
                then(dve.scalar_tensor_tensor(out=over, in0=bank[:, 1, 0:NE], scalar=float(P * j), in1=over,
                                              op0=ALU.is_gt, op1=ALU.add))
            then(dve.tensor_tensor_scan(ovend, ones[:, 0:NE], over, 0.0, ALU.mult, ALU.add))
            then(dve.tensor_copy(g.ovn[:], ovend[:, NE - 1:NE]))
            then(dve.tensor_tensor(ovhot, bcast(iota48.unsqueeze(2), [P, 48, NE]),
                                   bcast(ovend.unsqueeze(1), [P, 48, NE]), ALU.is_ge))
            then(dve.tensor_reduce(ovef, ovhot, AX.X, ALU.add))
            then(dve.tensor_scalar(ovef, ovef, float(NE - 1), None, ALU.min))
            then(dve.tensor_copy(g.ovexp[:], ovef))
            then(dve.tensor_tensor(ovh2, ovhot, bcast(over.unsqueeze(1), [P, 48, NE]), ALU.mult))
            then(dve.tensor_reduce(g.shift[:], ovh2, AX.X, ALU.add))
            then(dve.tensor_tensor(g.shift[:], iota48, g.shift[:], ALU.subtract))
            then(dve.tensor_scalar(g.shift[:], g.shift[:], 1.0, float(P), ALU.add, ALU.mult))



RING = [YT0 + 8192, WOUT, 34816, 28672]
BIG = 20000.0


def expert_weights(g, i):
    return g.region(RING[i], KT, 512), g.region(RING[i] + 4096, 2, D)


def load_expert(g, sp, e, slot=None, sems=None):
    slot = e % 4 if slot is None else slot
    s = (sems or g.exp_in)[slot]
    wgu, wdn = expert_weights(g, slot)
    pick = (lambda w: w[0, e]) if isinstance(e, int) else (lambda w: w[0, bass.ds(e, 1)].rearrange("a n f -> (a n) f"))
    sp.dma_start(wgu[:, :, 0:FF], pick(g.ins["w_exp_gate"]).rearrange("(p k) f -> p k f", p=P)).then_inc(s, 16)
    sp.dma_start(wgu[:, :, FF:], pick(g.ins["w_exp_up"]).rearrange("(p k) f -> p k f", p=P)).then_inc(s, 16)
    sp.dma_start(wdn, pick(g.ins["w_exp_down"]).rearrange("(p k) f -> p k f", p=P)).then_inc(s, 16)


def experts(g):
    nc, sem, bank = g.nc, g.sem, g.bank
    w = expert_work(g)
    g.y_rows = nc.dram_tensor("y_rows", [TOPK * T, D], F32, kind="Internal").ap()
    names = "q lst list flag idx turned xTa xTb up silu hid hT hTr down ya yb clear".split()
    s = {n: sem("e_" + n) for n in names}
    gathered, stored = [sem("gathered0"), sem("gathered1")], [sem("stored0"), sem("stored1")]

    def val(i, c):
        return i * 4 + c

    def half(i, c):
        return i * 2 + c // 2

    def quarter(i, c):
        return i + c // 4

    def wait(eng, sem_, n):
        if not isinstance(n, int) or n > 0:
            eng.wait_ge(sem_, n)

    def run(eng, before, step, after):
        before()
        for c in range(4):
            step(0, c)
        with eng.Fori(1, NE // 4 - 1) as i:
            for c in range(4):
                step(i, c)
        for c in range(4):
            step(NE // 4 - 1, c)
        after()

    def has(i, c, d):
        return not isinstance(i, int) or 0 <= 4 * i + c + d < NE

    with nc.Block() as block:
        @block.sync
        def _(sp):
            def load(i, c):
                sp.wait_ge(s["down"], val(i, c) + 1)
                load_expert(g, sp, val(i, c) + 4, c)
            with sp.Fori(0, NE // 4 - 1) as i:
                for c in range(4):
                    load(i, c)

        @block.tensor
        def _(pe):
            def lists(i, c):
                pe.wait_ge(s["q"], val(i, c) + 1)
                wait(pe, s["list"], val(i, c))
                for m in range(NT):
                    mm = pe.matmul(bank[:, 7, 0:9], w.q[:, m, :], values_of(g, m, val(i, c)),
                                   start=(m == 0), stop=(m == NT - 1))
                mm.then_inc(s["lst"], 1)

            def turn(i, c):
                k = c % 2
                pe.wait_ge(gathered[k], (half(i, c) + 1) * 16)
                wait(pe, s["xTa"], val(i, c))
                wait(pe, s["xTb"], val(i, c))
                turn_rows(g, pe, w.x[k]).then_inc(s["turned"], 1)

            def up(i, c):
                pe.wait_ge(s["xTa"], val(i, c) + 1)
                pe.wait_ge(s["xTb"], val(i, c) + 1)
                pe.wait_ge(g.exp_in[c % 4], (quarter(i, c) + 1) * 48)
                wait(pe, s["hid"], val(i, c))
                up_products(g, pe, w.xT[c % 2], c % 4).then_inc(s["up"], 1)

            def turn_hidden(i, c):
                pe.wait_ge(s["hid"], val(i, c) + 1)
                wait(pe, s["hTr"], val(i, c))
                turn_hid(g, pe, w.hid).then_inc(s["hT"], 1)

            def down(i, c):
                pe.wait_ge(s["hTr"], val(i, c) + 1)
                wait(pe, s["ya"], val(i, c))
                wait(pe, s["yb"], val(i, c))
                down_products(g, pe, w.hidT, c % 4).then_inc(s["down"], 1)

            def before():
                pe.wait_ge(s["clear"], 2)
                lists(0, 0)
                lists(0, 1)
                turn(0, 0)

            def step(i, c):
                up(i, c)
                if has(i, c, -1):
                    down(i, c - 1)
                if has(i, c, 1):
                    turn(i, c + 1)
                if has(i, c, 2):
                    lists(i, c + 2)
                turn_hidden(i, c)

            run(pe, before, step, lambda: down(NE // 4 - 1, 3))

        @block.vector
        def _(dve):
            def select(i, c):
                wait(dve, s["lst"], val(i, c))
                select_rows(g, dve, w, g.iota[:], val(i, c)).then_inc(s["q"], 1)

            def index(i, c):
                dve.wait_ge(s["lst"], val(i, c) + 1)
                if has(i, c, -4):
                    dve.wait_ge(stored[c % 2], (half(i, c) - 1) * 16)
                list_rows(g, dve, w, c % 4).then_inc(s["list"], 1)
                dve.wait_ge(s["list"], val(i, c) + 1)
                index_flags(g, dve, w, c % 4).then_inc(s["flag"], 1)
                dve.wait_ge(s["flag"], val(i, c) + 1)
                index_rows(g, dve, w, c % 4).then_inc(s["idx"], 1)

            def turned(i, c):
                dve.wait_ge(s["turned"], val(i, c) + 1)
                if has(i, c, -2):
                    dve.wait_ge(s["up"], val(i, c) - 1)
                dve.tensor_copy(w.xT[c % 2][:, 4:8, :].rearrange("p k n -> p (k n)"),
                                bank[:, 1, :]).then_inc(s["xTb"], 1)

            def hidden(i, c):
                dve.wait_ge(s["silu"], val(i, c) + 1)
                wait(dve, s["hT"], val(i, c))
                dve.tensor_tensor(w.hid, w.silu, bank[:, 2, FF:], ALU.mult).then_inc(s["hid"], 1)

            def result(i, c):
                dve.wait_ge(s["down"], val(i, c) + 1)
                if has(i, c, -2):
                    dve.wait_ge(stored[c % 2], half(i, c) * 16)
                dve.tensor_scalar(w.y[c % 2][:, HALF:], bank[:, 5, :], w.list[:, c % 4, 2:3], None,
                                  ALU.mult).then_inc(s["yb"], 1)

            def before():
                select(0, 0)
                index(0, 0)
                select(0, 1)
                index(0, 1)
                turned(0, 0)

            def step(i, c):
                hidden(i, c)
                if has(i, c, 2):
                    select(i, c + 2)
                if has(i, c, -1):
                    result(i, c - 1)
                if has(i, c, 1):
                    turned(i, c + 1)
                if has(i, c, 2):
                    index(i, c + 2)

            run(dve, before, step, lambda: result(NE // 4 - 1, 3))

        @block.scalar
        def _(act):
            def turned(i, c):
                act.wait_ge(s["turned"], val(i, c) + 1)
                if has(i, c, -2):
                    act.wait_ge(s["up"], val(i, c) - 1)
                act.activation(w.xT[c % 2][:, 0:4, :].rearrange("p k n -> p (k n)"), bank[:, 0, :],
                               ACT.Copy).then_inc(s["xTa"], 1)

            def gate(i, c):
                act.wait_ge(s["up"], val(i, c) + 1)
                wait(act, s["hid"], val(i, c))
                act.activation(w.silu, bank[:, 2, 0:FF], ACT.Silu).then_inc(s["silu"], 1)

            def hidden(i, c):
                act.wait_ge(s["hT"], val(i, c) + 1)
                wait(act, s["down"], val(i, c))
                act.activation(w.hidT.rearrange("p k n -> p (k n)"), bank[:, 3, 0:FF], ACT.Copy).then_inc(s["hTr"], 1)

            def result(i, c):
                act.wait_ge(s["down"], val(i, c) + 1)
                if has(i, c, -2):
                    act.wait_ge(stored[c % 2], half(i, c) * 16)
                act.activation(w.y[c % 2][:, 0:HALF], bank[:, 4, :], ACT.Copy,
                               scale=w.list[:, c % 4, 2:3]).then_inc(s["ya"], 1)

            def step(i, c):
                gate(i, c)
                if has(i, c, -1):
                    result(i, c - 1)
                if has(i, c, 1):
                    turned(i, c + 1)
                hidden(i, c)

            run(act, lambda: turned(0, 0), step, lambda: result(NE // 4 - 1, 3))

        @block.gpsimd
        def _(pool):
            w.bounds = g.bounds = transfer_bounds(pool)
            for k in range(2):
                pool.memset(w.x[k], 0.0).then_inc(s["clear"], 1)

            def gather(i, c):
                k = c % 2
                pool.wait_ge(s["idx"], val(i, c) + 1)
                if has(i, c, -2):
                    pool.wait_ge(s["turned"], val(i, c) - 1)
                gather_rows(g, pool, w, k, c % 4).then_inc(gathered[k], 16)

            def scatter(i, c):
                pool.wait_ge(s["ya"], val(i, c) + 1)
                pool.wait_ge(s["yb"], val(i, c) + 1)
                scatter_rows(g, pool, w, c % 2, c % 4).then_inc(stored[c % 2], 16)

            def before():
                pool.wait_ge(s["clear"], 2)
                for k in range(2):
                    pool.wait_ge(g.h1_stored[k], 16 * NT // 2)
                gather(0, 0)
                gather(0, 1)

            def step(i, c):
                if has(i, c, -1):
                    scatter(i, c - 1)
                if has(i, c, 2):
                    gather(i, c + 2)

            def after():
                scatter(NE // 4 - 1, 3)
                for k in range(2):
                    pool.wait_ge(stored[k], 16 * NE // 2)

            run(pool, before, step, after)


def expert_work(g):
    at = [0]

    def take(*dims):
        ap = g.region(at[0], *dims)
        at[0] += int(np.prod(dims))
        assert at[0] <= KT * T
        return ap

    w = Shared()
    w.x = [take(D) for _ in range(2)]
    w.xT = [take(KT, P) for _ in range(2)]
    w.y = [take(D) for _ in range(2)]
    w.q = take(NT * P // 2).bitcast(BF16).rearrange("p (m n) -> p m n", m=NT)
    w.silu, w.hid, w.hidT = take(FF), take(FF), take(2, P)
    w.index, w.list, w.flag = g.index, g.list, g.flag
    return w


def values_of(g, m, e):
    if isinstance(e, int):
        return g.values[:, m, e].rearrange("p v k -> p (v k)")
    return g.values[:, m, bass.ds(e, 1)].rearrange("p a v k -> p (a v k)")


def select_rows(g, dve, w, places, e):
    pos = g.pos[:, :, e:e + 1] if isinstance(e, int) else g.pos[:, :, bass.ds(e, 1)]
    return dve.tensor_tensor(w.q, bcast(places.unsqueeze(1), [P, NT, P]), bcast(pos, [P, NT, P]), ALU.is_equal)


def list_rows(g, dve, w, b):
    return dve.tensor_reduce(w.list[:, b, :], g.bank[:, 7, 0:9].rearrange("p (v k) -> p v k", v=3), AX.X, ALU.add)


def index_flags(g, dve, w, b):
    return dve.tensor_scalar(w.flag[:], w.list[:, b, 0:2], 0.0, BIG, ALU.is_equal, ALU.mult)


def index_rows(g, dve, w, b):
    return dve.scalar_tensor_tensor(out=w.index[:, b, :], in0=w.list[:, b, 0:2], scalar=-1.0, in1=w.flag[:],
                                    op0=ALU.add, op1=ALU.add)


def transfer_bounds(pool):
    first, last = pool.alloc_register("first_row"), pool.alloc_register("last_row")
    pool.reg_mov(first, 0)
    return first, last


def gather_rows(g, pool, w, k, b):
    first, last = w.bounds
    pool.reg_add(last, first, T - 1)
    return pool.indirect_dma_start(w.x[k], None, g.h1_rows, bass.IndirectOffsetOnAxis(ap=w.index[:, b, 0:1], axis=0),
                                   bounds_check=last, oob_is_err=False)


def scatter_rows(g, pool, w, k, b):
    first, last = w.bounds
    pool.reg_add(last, first, TOPK * T - 1)
    return pool.indirect_dma_start(g.y_rows, bass.IndirectOffsetOnAxis(ap=w.index[:, b, 1:2], axis=0), w.y[k], None,
                                   bounds_check=last, oob_is_err=False)


def turn_rows(g, pe, x):
    cols = x.rearrange("p (n k) -> p k n", k=KT)
    for k in range(KT):
        mm = pe.transpose(g.bank[:, k // 4, (k % 4) * P:(k % 4 + 1) * P], cols[:, k, :], g.ident[:])
    return mm


def up_products(g, pe, xT, slot):
    wgu, _ = expert_weights(g, slot)
    for k in range(KT):
        mm = pe.matmul(g.bank[:, 2, :], xT[:, k, :], wgu[:, k, :], start=(k == 0), stop=(k == KT - 1))
    return mm


def turn_hid(g, pe, hid):
    cols = hid.rearrange("p (n k) -> p k n", k=2)
    for k in range(2):
        mm = pe.transpose(g.bank[:, 3, k * P:(k + 1) * P], cols[:, k, :], g.ident[:])
    return mm


def down_products(g, pe, hidT, slot):
    _, wdn = expert_weights(g, slot)
    for h in range(2):
        for k in range(2):
            mm = pe.matmul(g.bank[:, 4 + h, :], hidT[:, k, :], wdn[:, k, h * HALF:(h + 1) * HALF],
                           start=(k == 0), stop=(k == 1))
    return mm


def overflow(g):
    nc, sem, bank = g.nc, g.sem, g.bank
    w = expert_work(g)
    names = "places q lst list flag idx turned xTa xTb up silu hid hT hTr down ya yb gathered stored free".split()
    s = {n: sem("v_" + n) for n in names}
    places = g.region(LISTS, P)
    loaded = [sem("v_loaded")]

    def blocks(eng, body, table=True):
        n = eng.value_load(g.ovn[0:1, 0:1], min_val=0, max_val=OVER)
        with eng.Fori(0, n) as o:
            e = eng.value_load(g.ovexp[0:1, bass.ds(o, 1)], min_val=0, max_val=NE - 1) if table else None
            body(o, e)

    with nc.Block() as block:
        @block.sync
        def _(sp):
            def body(o, e):
                sp.wait_ge(s["down"], o + 1)
                load_expert(g, sp, e, 0, loaded)
            blocks(sp, body)

        @block.vector
        def _(dve):
            def body(o, e):
                dve.wait_ge(s["free"], o + 1)
                dve.tensor_scalar(places, g.iota[:], g.shift[:, bass.ds(o, 1)], None, ALU.add).then_inc(s["places"], 1)
                dve.wait_ge(s["places"], o + 1)
                select_rows(g, dve, w, places, e).then_inc(s["q"], 1)
                dve.wait_ge(s["lst"], o + 1)
                list_rows(g, dve, w, 0).then_inc(s["list"], 1)
                dve.wait_ge(s["list"], o + 1)
                index_flags(g, dve, w, 0).then_inc(s["flag"], 1)
                dve.wait_ge(s["flag"], o + 1)
                index_rows(g, dve, w, 0).then_inc(s["idx"], 1)
                dve.wait_ge(s["turned"], o + 1)
                dve.tensor_copy(w.xT[0][:, 4:8, :].rearrange("p k n -> p (k n)"), bank[:, 1, :]).then_inc(s["xTb"], 1)
                dve.wait_ge(s["silu"], o + 1)
                dve.tensor_tensor(w.hid, w.silu, bank[:, 2, FF:], ALU.mult).then_inc(s["hid"], 1)
                dve.wait_ge(s["down"], o + 2)
                dve.tensor_scalar(w.y[0][:, HALF:], bank[:, 5, :], w.list[:, 0, 2:3], None, ALU.mult).then_inc(s["yb"], 1)
            blocks(dve, body)

        @block.tensor
        def _(pe):
            def body(o, e):
                pe.wait_ge(s["q"], o + 1)
                for m in range(NT):
                    mm = pe.matmul(bank[:, 7, 0:9], w.q[:, m, :], values_of(g, m, e),
                                   start=(m == 0), stop=(m == NT - 1))
                mm.then_inc(s["lst"], 1)
                pe.wait_ge(s["gathered"], (o + 1) * 16)
                turn_rows(g, pe, w.x[0]).then_inc(s["turned"], 1)
                pe.wait_ge(s["xTa"], o + 1)
                pe.wait_ge(s["xTb"], o + 1)
                pe.wait_ge(loaded[0], (o + 1) * 48)
                up_products(g, pe, w.xT[0], 0).then_inc(s["up"], 1)
                pe.wait_ge(s["hid"], o + 1)
                turn_hid(g, pe, w.hid).then_inc(s["hT"], 1)
                pe.wait_ge(s["hTr"], o + 1)
                down_products(g, pe, w.hidT, 0).then_inc(s["down"], 1)
                pe.wait_ge(s["ya"], o + 1)
                pe.wait_ge(s["yb"], o + 1)
            pe.sem_inc(s["down"], 1)
            blocks(pe, body)

        @block.scalar
        def _(act):
            def body(o, e):
                act.wait_ge(s["turned"], o + 1)
                act.activation(w.xT[0][:, 0:4, :].rearrange("p k n -> p (k n)"), bank[:, 0, :],
                               ACT.Copy).then_inc(s["xTa"], 1)
                act.wait_ge(s["up"], o + 1)
                act.activation(w.silu, bank[:, 2, 0:FF], ACT.Silu).then_inc(s["silu"], 1)
                act.wait_ge(s["hT"], o + 1)
                act.activation(w.hidT.rearrange("p k n -> p (k n)"), bank[:, 3, 0:FF], ACT.Copy).then_inc(s["hTr"], 1)
                act.wait_ge(s["down"], o + 2)
                act.activation(w.y[0][:, 0:HALF], bank[:, 4, :], ACT.Copy, scale=w.list[:, 0, 2:3]).then_inc(s["ya"], 1)
            blocks(act, body, False)

        @block.gpsimd
        def _(pool):
            w.bounds = g.bounds

            def body(o, e):
                pool.wait_ge(s["idx"], o + 1)
                gather_rows(g, pool, w, 0, 0).then_inc(s["gathered"], 16)
                pool.wait_ge(s["ya"], o + 1)
                pool.wait_ge(s["yb"], o + 1)
                scatter_rows(g, pool, w, 0, 0).then_inc(s["stored"], 16)
                pool.wait_ge(s["stored"], (o + 1) * 16)
                pool.sem_inc(s["free"], 1)
            pool.sem_inc(s["free"], 1)
            blocks(pool, body, False)



def finish(g):
    nc, sem = g.nc, g.sem
    rows = [g.region(YT0 + 8192 + TOPK * D * i, TOPK, D) for i in range(3)]
    g2, b2 = g.region(0, D), g.region(D, D)
    res = [g.region(2 * D + D * i, D) for i in range(2)]
    base = g.base
    stats, mv, rstd = g.stats, g.mv, g.rstd
    names = "gb pa pb a b c d st ag ve sd rs xn g2 b2".split()
    s = {n: sem("f_" + n) for n in names}
    rows_in = [sem(f"rows_in{i}") for i in range(3)]
    out_done = [sem("out_done0"), sem("out_done1")]
    y = g.y_rows.rearrange("(k m p) d -> m p k d", k=TOPK, p=P)

    def store(act, m):
        act.wait_ge(s["b2"], m + 1)
        act.dma_start(g.out[0, m * P:(m + 1) * P, :], res[m % 2]).then_inc(out_done[m % 2], 16)

    with nc.Block() as block:
        @block.sync
        def _(sp):
            for dst, src in ((g2, g.ins["ln2_g"][0]), (b2, g.ins["ln2_b"][0])):
                sp.dma_start(dst, src.rearrange("(a n) -> a n", a=1).to_broadcast([P, D])).then_inc(s["gb"], 16)
            for m in range(NT):
                if m >= 3:
                    sp.wait_ge(s["d"], m - 2)
                sp.dma_start(rows[m % 3], y[m]).then_inc(rows_in[m % 3], 16)

        @block.gpsimd
        def _(pool):
            pool.wait_ge(s["gb"], 32)

            def half_sum(m):
                r = rows[m % 3]
                pool.wait_ge(rows_in[m % 3], 16 * (m // 3 + 1))
                pool.tensor_tensor(r[:, 3, :], r[:, 3, :], r[:, 4, :], ALU.add).then_inc(s["pa"], 1)
                pool.wait_ge(s["pa"], m + 1)
                pool.tensor_tensor(r[:, 3, :], r[:, 3, :], r[:, 5, :], ALU.add).then_inc(s["pb"], 1)

            half_sum(0)
            for m in range(NT):
                if m + 1 < NT:
                    half_sum(m + 1)
                o = res[m % 2]
                pool.wait_ge(s["xn"], m + 1)
                pool.tensor_tensor(o, o, g2, ALU.mult).then_inc(s["g2"], 1)
                pool.wait_ge(s["g2"], m + 1)
                pool.tensor_tensor(o, o, b2, ALU.add).then_inc(s["b2"], 1)

        @block.vector
        def _(dve):
            for m in range(NT):
                r, z = rows[m % 3], base[:, m, :]
                dve.wait_ge(rows_in[m % 3], 16 * (m // 3 + 1))
                dve.tensor_tensor(z, z, r[:, 0, :], ALU.add).then_inc(s["a"], 1)
                dve.wait_ge(s["a"], m + 1)
                dve.tensor_tensor(z, z, r[:, 1, :], ALU.add).then_inc(s["b"], 1)
                dve.wait_ge(s["b"], m + 1)
                dve.tensor_tensor(z, z, r[:, 2, :], ALU.add).then_inc(s["c"], 1)
                dve.wait_ge(s["c"], m + 1)
                dve.wait_ge(s["pb"], m + 1)
                dve.tensor_tensor(z, z, r[:, 3, :], ALU.add).then_inc(s["d"], 1)
                dve.wait_ge(s["d"], m + 1)
                for h in range(2):
                    dve.bn_stats(stats[:, h, :], z[:, h * HALF:(h + 1) * HALF]).then_inc(s["st"], 1)
                dve.wait_ge(s["st"], 2 * m + 2)
                dve.bn_aggr(mv[:], stats[:]).then_inc(s["ag"], 1)
                dve.wait_ge(s["ag"], m + 1)
                dve.tensor_scalar(rstd[:], mv[:, 1:2], LN_EPS, None, ALU.add).then_inc(s["ve"], 1)
                dve.wait_ge(s["sd"], m + 1)
                dve.reciprocal(rstd[:], rstd[:]).then_inc(s["rs"], 1)
                dve.wait_ge(s["rs"], m + 1)
                if m >= 2:
                    dve.wait_ge(out_done[m % 2], 16 * (m // 2))
                dve.tensor_scalar(res[m % 2], z, mv[:, 0:1], rstd[:], ALU.subtract, ALU.mult).then_inc(s["xn"], 1)

        @block.scalar
        def _(act):
            for m in range(NT):
                act.wait_ge(s["ve"], m + 1)
                act.activation(rstd[:], rstd[:], ACT.Sqrt).then_inc(s["sd"], 1)
                if m:
                    store(act, m - 1)
            store(act, NT - 1)
            for k in range(2):
                act.wait_ge(out_done[k], 16 * NT // 2)


def layer(nc, ins, out):
    with ExitStack() as ctx:
        g = setup(nc, ctx, ins)
        g.out = out
        plan_slots(g)
        norm_in(g)
        project(g)
        mix_a(g)
        mix_b(g)
        mix_c(g)
        mix_d(g)
        g.release()
        merge(g)
        out_norm(g)
        route(g)
        g.release()
        experts(g)
        overflow(g)
        finish(g)


_INS = ['x', 'ln_in_g', 'ln_in_b', 'w_in', 'a_sinks', 'rel_bias', 'b_lower_bounds', 'b_norm_w', 'c_conv_w',
        'c_conv_b', 'c_dt_bias', 'c_a_log', 'c_d_skip', 'c_norm_w', 'd_f_bias', 'w_br_a', 'w_br_b', 'w_br_c',
        'w_br_d', 'w_out', 'ln1_g', 'ln1_b', 'w_router', 'router_bias', 'w_exp_gate', 'w_exp_up', 'w_exp_down',
        'w_sh_gate', 'w_sh_up', 'w_sh_down', 'ln2_g', 'ln2_b']


def bucket_onehot():
    rel = np.arange(256) - 127
    n = np.abs(rel)
    large = 8 + (np.log(np.maximum(n, 1) / 8) / np.log(128 / 8) * 8).astype(np.int32)
    bucket = (rel > 0) * 16 + np.where(n < 8, n, np.minimum(large, 15))
    return (bucket[None, :] == np.arange(32)[:, None]).astype(np.float32)


def kernel(**inputs):
    import numpy as _np
    import concourse.bacc as _bacc
    from concourse import mybir as _mybir
    from concourse.bass_utils import run_bass_kernel_spmd as _run

    nc = _bacc.Bacc("TRN2", target_bir_lowering=False, num_devices=1)
    arrays, args = {}, {}
    given = {name: inputs[name] for name in _INS}
    given["bucket_onehot"] = bucket_onehot()
    given["zero4"] = _np.zeros(4, _np.float32)
    for name, a in given.items():
        a = _np.ascontiguousarray(a)
        arrays[f"in_{name}_dram"] = a
        args[name] = nc.dram_tensor(f"in_{name}_dram", a.shape, _mybir.dt.from_np(a.dtype),
                                    kind="ExternalInput").ap()
    out = nc.dram_tensor("out_0_dram", (1, T, D), F32, kind="ExternalOutput").ap()
    layer(nc, args, out)
    r = _run(nc, [arrays], core_ids=[0])
    return r.results[0]["out_0_dram"]
```
